# Optimizing a Trainium2 kernel written in Bass

```python
import math
import jax
import jax.numpy as jnp
from jax import lax
import numpy as np

D_MODEL = 1024
BATCH = 1
SEQ = 512
DEPTH = 2

HEAD_DIM = 64
ROT_DIM = HEAD_DIM // 4
ROPE_THETA = 500000.0
A_GROUPS = ((128, 1), (512, 4), (2048, 16))
A_HEADS = 8
B_HEADS = D_MODEL // (2 * HEAD_DIM)
D_FF = ((8 * D_MODEL // 3 + 255) // 256) * 256
CONV_WIDTH = 3
Q_BLOCK = 128
N_A_LAYERS = DEPTH // 2
N_B_LAYERS = DEPTH - N_A_LAYERS
NORM_EPS = 1e-6
SUBLN_EPS = 1e-5
NEG_INF = -1e30

kernel_name = "yoco_dilated_diffattn_convffn_block"

def rms_norm(x, g, eps=NORM_EPS):
    x32 = x.astype(jnp.float32)
    y = x32 * lax.rsqrt(jnp.mean(x32 * x32, axis=-1, keepdims=True) + eps)
    return (y * g.astype(jnp.float32)).astype(x.dtype)

def ada_mod(c_act, w, b, n):
    m = c_act @ w + b
    return jnp.split(m[:, None, :], n, axis=-1)

def rope_tables(positions):
    inv = jnp.power(ROPE_THETA, -jnp.arange(0, ROT_DIM, 2, dtype=jnp.float32) / ROT_DIM)
    ang = positions.astype(jnp.float32)[..., None] * inv
    return jnp.cos(ang), jnp.sin(ang)

def apply_partial_rope(x, cos, sin):
    extra = x.ndim - 3
    shp = cos.shape[:2] + (1,) * extra + cos.shape[-1:]
    cos = cos.reshape(shp).astype(x.dtype)
    sin = sin.reshape(shp).astype(x.dtype)
    half = ROT_DIM // 2
    x1 = x[..., :half]
    x2 = x[..., half:ROT_DIM]
    return jnp.concatenate([x1 * cos - x2 * sin, x2 * cos + x1 * sin, x[..., ROT_DIM:]], axis=-1)

def dilated_window_attention(q, k, v, window, dilation):
    B, S, H, Dh = q.shape
    L = S // dilation
    W = window // dilation
    nb = -(-L // W)
    Lp = nb * W

    def by_residue(t):
        return t.reshape(B, L, dilation, H, Dh).transpose(0, 2, 1, 3, 4)

    qr, kr, vr = by_residue(q), by_residue(k), by_residue(v)
    qb = jnp.pad(qr, ((0, 0), (0, 0), (0, Lp - L), (0, 0), (0, 0))).reshape(B, dilation, nb, W, H, Dh)

    def kv_blocks(t):
        tb = jnp.pad(t, ((0, 0), (0, 0), (W, Lp - L), (0, 0), (0, 0))).reshape(B, dilation, nb + 1, W, H, Dh)
        return jnp.concatenate([tb[:, :, :-1], tb[:, :, 1:]], axis=3)

    kb, vb = kv_blocks(kr), kv_blocks(vr)
    i = jnp.arange(W)[:, None]
    j = jnp.arange(2 * W)[None, :]
    n = jnp.arange(nb)[:, None, None]
    delta = W + i - j
    mask = (delta >= 0) & (delta <= W) & (n * W + j - W >= 0)

    s = jnp.einsum('brnqhd,brnkhd->brnhqk', qb, kb).astype(jnp.float32) * (Dh ** -0.5)
    s = jnp.where(mask[None, None, :, None], s, NEG_INF)
    mx = jnp.max(s, axis=-1, keepdims=True)
    p = jnp.exp(s - mx)
    den = jnp.sum(p, axis=-1)
    o = jnp.einsum('brnhqk,brnkhd->brnqhd', p.astype(v.dtype), vb).astype(jnp.float32)
    o = o / jnp.transpose(den, (0, 1, 2, 4, 3))[..., None]
    lse = jnp.transpose(mx[..., 0] + jnp.log(den), (0, 1, 2, 4, 3))

    def back(t):
        t = t.reshape((B, dilation, Lp) + t.shape[4:])[:, :, :L]
        t = jnp.moveaxis(t, 1, 2)
        return t.reshape((B, S) + t.shape[3:])

    return back(o), back(lse)

def dilated_mixer(h, w_qkv, w_o, cos, sin):
    B, S, _ = h.shape
    qkv = (h @ w_qkv).reshape(B, S, len(A_GROUPS), 3, A_HEADS, HEAD_DIM)
    outs, lses = [], []
    for g, (window, dil) in enumerate(A_GROUPS):
        q = apply_partial_rope(qkv[:, :, g, 0], cos, sin)
        k = apply_partial_rope(qkv[:, :, g, 1], cos, sin)
        o, lse = dilated_window_attention(q, k, qkv[:, :, g, 2], window, dil)
        outs.append(o)
        lses.append(lse)
    o = jnp.stack(outs, axis=0)
    alpha = jax.nn.softmax(jnp.stack(lses, axis=0), axis=0)
    mixed = jnp.sum(alpha[..., None] * o, axis=0)
    return mixed.reshape(B, S, A_HEADS * HEAD_DIM).astype(h.dtype) @ w_o

def shared_kv(x, c_act, kv_norm, kv_mod_w, kv_mod_b, w_k, w_v, cos, sin):
    B, S, _ = x.shape
    shift, scale = ada_mod(c_act, kv_mod_w, kv_mod_b, 2)
    hk = rms_norm(x, kv_norm) * (1.0 + scale) + shift
    k = apply_partial_rope((hk @ w_k).reshape(B, S, B_HEADS, 2, HEAD_DIM), cos, sin)
    v = (hk @ w_v).reshape(B, S, B_HEADS, 2 * HEAD_DIM)
    return k, v

def diff_attention(q, k, v, lam):
    B, S, H, _, Dh = q.shape
    nq = S // Q_BLOCK
    qb = q.reshape(B, nq, Q_BLOCK, H, 2, Dh).transpose(1, 0, 2, 3, 4, 5)
    kpos = jnp.arange(S)
    scale = Dh ** -0.5

    def one_block(args):
        qi, bi = args
        s = jnp.einsum('bqhcd,bkhcd->bhcqk', qi, k).astype(jnp.float32) * scale
        qpos = bi * Q_BLOCK + jnp.arange(Q_BLOCK)
        s = jnp.where((kpos[None, :] <= qpos[:, None])[None, None, None], s, NEG_INF)
        p = jax.nn.softmax(s, axis=-1)
        a = p[:, :, 0] - lam * p[:, :, 1]
        return jnp.einsum('bhqk,bkhe->bqhe', a.astype(v.dtype), v)

    o = lax.map(one_block, (qb, jnp.arange(nq)))
    return o.transpose(1, 0, 2, 3, 4).reshape(B, S, H, 2 * Dh)

def diff_mixer(h, k, v, w_q, lq1, lk1, lq2, lk2, subln, w_o, lam_init, cos, sin):
    B, S, _ = h.shape
    q = apply_partial_rope((h @ w_q).reshape(B, S, B_HEADS, 2, HEAD_DIM), cos, sin)
    f32 = jnp.float32
    lam = (jnp.exp(jnp.sum(lq1.astype(f32) * lk1.astype(f32)))
           - jnp.exp(jnp.sum(lq2.astype(f32) * lk2.astype(f32))) + lam_init)
    o = diff_attention(q, k, v, lam)
    o = rms_norm(o, subln, eps=SUBLN_EPS) * (1.0 - lam_init)
    return o.reshape(B, S, B_HEADS * 2 * HEAD_DIM) @ w_o

def conv_ffn(h, w_gate, w_up, conv_w, conv_b, w_down):
    S = h.shape[1]
    a = h @ w_gate
    ap = jnp.pad(a, ((0, 0), (CONV_WIDTH - 1, 0), (0, 0)))
    conv = conv_b
    for t in range(CONV_WIDTH):
        conv = conv + conv_w[t] * ap[:, t:t + S]
    return (jax.nn.gelu(conv, approximate=True) * (h @ w_up)) @ w_down

def setup_inputs(seed: int = 0) -> dict:
    key = jax.random.key(seed)
    ks = jax.random.split(key, 32)
    f32 = jnp.float32
    D, F = D_MODEL, D_FF
    G = len(A_GROUPS)
    a_inner = A_HEADS * HEAD_DIM
    b_inner = B_HEADS * 2 * HEAD_DIM

    def w(k, shape, fan_in, gain=1.0):
        return jax.random.normal(k, shape, f32) * (gain * fan_in ** -0.5)

    def gain(k, shape):
        return 1.0 + 0.05 * jax.random.normal(k, shape, f32)

    def bias(k, shape):
        return 0.01 * jax.random.normal(k, shape, f32)

    positions = (jnp.arange(SEQ, dtype=jnp.int32)[None, :]
                 + jax.random.randint(ks[2], (BATCH, 1), 0, 2048, dtype=jnp.int32))
    return {
        'x': jax.random.normal(ks[0], (BATCH, SEQ, D), f32),
        'c': jax.random.normal(ks[1], (BATCH, D), f32),
        'positions': positions,
        'mod_mix_w': w(ks[3], (DEPTH, D, 3 * D), D, 0.5),
        'mod_mix_b': bias(ks[4], (DEPTH, 3 * D)),
        'mod_ffn_w': w(ks[5], (DEPTH, D, 3 * D), D, 0.5),
        'mod_ffn_b': bias(ks[6], (DEPTH, 3 * D)),
        'norm_pre_mix': gain(ks[7], (DEPTH, D)),
        'norm_post_mix': gain(ks[8], (DEPTH, D)),
        'norm_pre_ffn': gain(ks[9], (DEPTH, D)),
        'norm_post_ffn': gain(ks[10], (DEPTH, D)),
        'ffn_w_gate': w(ks[11], (DEPTH, D, F), D),
        'ffn_w_up': w(ks[12], (DEPTH, D, F), D),
        'ffn_conv_w': w(ks[13], (DEPTH, CONV_WIDTH, F), CONV_WIDTH),
        'ffn_conv_b': bias(ks[14], (DEPTH, F)),
        'ffn_w_down': w(ks[15], (DEPTH, F, D), F),
        'a_w_qkv': w(ks[16], (N_A_LAYERS, D, G * 3 * a_inner), D),
        'a_w_o': w(ks[17], (N_A_LAYERS, a_inner, D), a_inner),
        'kv_norm': gain(ks[18], (D,)),
        'kv_mod_w': w(ks[19], (D, 2 * D), D, 0.5),
        'kv_mod_b': bias(ks[20], (2 * D,)),
        'b_w_k': w(ks[21], (D, b_inner), D),
        'b_w_v': w(ks[22], (D, b_inner), D),
        'b_w_q': w(ks[23], (N_B_LAYERS, D, b_inner), D),
        'b_lambda_q1': 0.1 * jax.random.normal(ks[24], (N_B_LAYERS, HEAD_DIM), f32),
        'b_lambda_k1': 0.1 * jax.random.normal(ks[25], (N_B_LAYERS, HEAD_DIM), f32),
        'b_lambda_q2': 0.1 * jax.random.normal(ks[26], (N_B_LAYERS, HEAD_DIM), f32),
        'b_lambda_k2': 0.1 * jax.random.normal(ks[27], (N_B_LAYERS, HEAD_DIM), f32),
        'b_subln': gain(ks[28], (N_B_LAYERS, 2 * HEAD_DIM)),
        'b_w_o': w(ks[29], (N_B_LAYERS, b_inner, D), b_inner),
    }

def reference(x, c, positions, mod_mix_w, mod_mix_b, mod_ffn_w, mod_ffn_b,
              norm_pre_mix, norm_post_mix, norm_pre_ffn, norm_post_ffn,
              ffn_w_gate, ffn_w_up, ffn_conv_w, ffn_conv_b, ffn_w_down,
              a_w_qkv, a_w_o, kv_norm, kv_mod_w, kv_mod_b, b_w_k, b_w_v,
              b_w_q, b_lambda_q1, b_lambda_k1, b_lambda_q2, b_lambda_k2, b_subln, b_w_o):
    c_act = jax.nn.silu(c)
    cos, sin = rope_tables(positions)
    k_sh, v_sh = None, None
    for l in range(DEPTH):
        shift, scale, gate = ada_mod(c_act, mod_mix_w[l], mod_mix_b[l], 3)
        if l == N_A_LAYERS:
            k_sh, v_sh = shared_kv(x, c_act, kv_norm, kv_mod_w, kv_mod_b, b_w_k, b_w_v, cos, sin)
        h = rms_norm(x, norm_pre_mix[l]) * (1.0 + scale) + shift
        if l < N_A_LAYERS:
            y = dilated_mixer(h, a_w_qkv[l], a_w_o[l], cos, sin)
        else:
            j = l - N_A_LAYERS
            lam_init = 0.8 - 0.6 * math.exp(-0.3 * l)
            y = diff_mixer(h, k_sh, v_sh, b_w_q[j], b_lambda_q1[j], b_lambda_k1[j],
                           b_lambda_q2[j], b_lambda_k2[j], b_subln[j], b_w_o[j], lam_init, cos, sin)
        x = x + gate * rms_norm(y, norm_post_mix[l])
        shift, scale, gate = ada_mod(c_act, mod_ffn_w[l], mod_ffn_b[l], 3)
        h = rms_norm(x, norm_pre_ffn[l]) * (1.0 + scale) + shift
        y = conv_ffn(h, ffn_w_gate[l], ffn_w_up[l], ffn_conv_w[l], ffn_conv_b[l], ffn_w_down[l])
        x = x + gate * rms_norm(y, norm_post_ffn[l])
    return x


_drawn_inputs = setup_inputs


def setup_inputs(seed=0):
    import zlib

    import numpy as np

    out = dict(_drawn_inputs(seed))
    spreads = {}
    factors = {'mod_mix_b': 3.181,
     'mod_ffn_b': 3.834,
     'norm_pre_mix': 2.885,
     'norm_post_ffn': 3.098,
     'ffn_conv_b': 8.0,
     'kv_norm': 4.428,
     'kv_mod_b': 8.0,
     'b_lambda_q1': 8.0,
     'b_lambda_k1': 8.0,
     'b_subln': 3.871}
    for name, (base, spread) in spreads.items():
        noise = np.random.default_rng([zlib.crc32(name.encode()), seed]).standard_normal(out[name].shape)
        drawn = base * np.exp(spread * noise) if base else spread * noise
        out[name] = jnp.asarray(drawn.astype(out[name].dtype))
    for name, factor in factors.items():
        out[name] = (out[name] * factor).astype(out[name].dtype)
    return out
```

```python
import math
from contextlib import ExitStack

import numpy as np
import concourse.bass as bass
from concourse import mybir

F32 = mybir.dt.float32
F32R = mybir.dt.float32r
BF16 = mybir.dt.bfloat16
I32 = mybir.dt.int32
ALU = mybir.AluOpType
ACT = mybir.ActivationFunctionType
AX = mybir.AxisListType

P = 128
HEAD_DIM = 64
ROT_HALF = HEAD_DIM // 8
ROPE_THETA = 500000.0
NORM_EPS = 1e-6
SUBLN_EPS = 1e-5
MASKED = -1e30
SCORE_SCALE = HEAD_DIM ** -0.5
LAYER_B = 1
LAM_INIT = 0.8 - 0.6 * math.exp(-0.3 * LAYER_B)
CLASSES = 4
WINDOW = 128


class Signal:

    def __init__(self, nc, ctx, name, stream, k=1, step=1, before=0):
        self.sems = [ctx.enter_context(nc.semaphore(f"{name}{j}" if k > 1 else name)) for j in range(k)]
        self.stream, self.k, self.step, self.before = stream, k, step, before


class Count:

    def __init__(self, eng):
        self.eng, self.n, self.turn, self.per = eng, {}, None, {}

    def _number(self, sig, ahead, more):
        event = self.n.get(sig.stream, 0) + ahead
        value = sig.step * (event // sig.k + more + sig.before)
        if self.turn is None:
            return sig.sems[event % sig.k], max(value, 0)
        per = self.per.get(sig.stream, 0)
        assert per % sig.k == 0 and value > 0, (sig.stream, per, event)
        return sig.sems[event % sig.k], (self.turn * (per // sig.k * sig.step) + value if per else value)

    def done(self, sig, ahead=0):
        return self._number(sig, ahead, 1)

    def here(self, sig, ahead=0):
        event = self.n.get(sig.stream, 0) + ahead
        return sig.sems[event % sig.k], sig.step

    def at(self, stream, k):
        assert self.turn is None or self.per.get(stream, 0) % k == 0, (stream, k)
        return self.n.get(stream, 0) % k

    def passed(self, stream, events=1):
        self.n[stream] = self.n.get(stream, 0) + events

    def loop(self, turns, **per):
        return _Loop(self, turns, per)


class _Loop:
    def __init__(self, count, turns, per):
        self.count, self.turns, self.per = count, turns, per

    def __enter__(self):
        c = self.count
        self.start = dict(c.n)
        self.fori = c.eng.Fori(0, self.turns)
        c.turn, c.per = self.fori.__enter__(), self.per
        return c.turn

    def __exit__(self, *exc):
        c = self.count
        self.fori.__exit__(*exc)
        if exc[0] is not None:
            return False
        turned = {s: c.n[s] - self.start.get(s, 0) for s in c.n if c.n[s] != self.start.get(s, 0)}
        assert turned == {s: v for s, v in self.per.items() if v}, (turned, self.per)
        for s, v in turned.items():
            c.n[s] = self.start.get(s, 0) + self.turns * v
        c.turn, c.per = None, {}
        return False


def yoco_trunk(nc, x, c, positions, mod_mix_w, mod_mix_b, mod_ffn_w, mod_ffn_b,
               norm_pre_mix, norm_post_mix, norm_pre_ffn, norm_post_ffn,
               ffn_w_gate, ffn_w_up, ffn_conv_w, ffn_conv_b, ffn_w_down,
               a_w_qkv, a_w_o, kv_norm, kv_mod_w, kv_mod_b, b_w_k, b_w_v,
               b_w_q, b_lambda_q1, b_lambda_k1, b_lambda_q2, b_lambda_k2, b_subln, b_w_o, out):
    _, T, D = x.shape
    FF = ffn_w_gate.shape[2]
    DT = D // P
    FT = FF // P
    NT = T // P
    A_INNER = a_w_o.shape[1]
    PAIRS = A_INNER // P
    HEADS_B = b_w_q.shape[2] // P
    FT_TURN = 3
    MOD_TURNS = 6
    assert (T, D, NT) == (512, 1024, CLASSES) and FT == 22 and PAIRS == 4 and HEADS_B == 8

    MIX, FFN, KV = (0, 3 * DT), (6 * DT, 9 * DT), 12 * DT
    NMOD = 14 * DT
    C_ROW, PRE_MIX, POST_MIX, PRE_FFN, POST_FFN, KVN = 0, DT, 3 * DT, 5 * DT, 7 * DT, 9 * DT
    NVEC = 10 * DT
    CONV = 4 * FT

    with ExitStack() as ctx:
        def sb(name, shape, dt=F32, where=ctx):
            return where.enter_context(nc.sbuf_tensor(name, shape, dt))

        xT = sb("xT", [P, DT, T])
        raw = sb("raw", [P, 3, 1024])
        whi = sb("whi", [P, 3, 1024], F32R)
        wlo = sb("wlo", [P, 3, 1024], F32R)
        mraw = sb("mraw", [P, 2, DT, P])
        macc = sb("macc", [P, DT, P])
        identf = sb("identf", [P, P])
        onesf = sb("onesf", [P, P])
        identb = sb("identb", [P, P], BF16)
        band = sb("band", [P, 7 * P], BF16)
        near = sb("near", [P, 2 * P], BF16)
        causal = sb("causal", [P, T], BF16)
        cosT = sb("cosT", [P, T])
        sinT = sb("sinT", [P, T])
        vcol = sb("vcol", [P, NVEC])
        bcol = sb("bcol", [P, NMOD])
        modc = sb("modc", [P, NMOD])
        convc = sb("convc", [P, 2 * CONV])
        presc = sb("presc", [P, 5 * DT])
        postg = sb("postg", [P, 4 * DT])
        csil = sb("csil", [P, DT])
        small = sb("small", [P, 32])
        neghalf = sb("neghalf", [P, NT])
        marks = sb("marks", [P, 5])
        stat = sb("stat", [P, 3 * NT])
        tmp = sb("tmp", [P, 4, T])
        sqacc = sb("sqacc", [P, T])
        rb = sb("rb", [P, T])
        nmax = sb("nmax", [P, 2, 2])
        den = sb("den", [P, 4, 2])
        rden = sb("rden", [P, 2])
        FREQ, RMASK, RKEEP, RSIGN, SUBLN, NEGLAM, SUBG = range(7)
        STAT_V, STAT_R = small[:, 8:12], small[:, 12:16]
        EXPC = small[:, 16:24]
        MEAN_X, GAIN_X, STAT_Q = stat[:, 0:NT], stat[:, NT:2 * NT], stat[:, 2 * NT:3 * NT]

        ffn_mem, l0_mem, l1_mem = ExitStack(), ExitStack(), ExitStack()
        with ffn_mem:
            hhi = sb("hhi", [P, DT, T], F32R, ffn_mem)
            hlo = sb("hlo", [P, DT, T], F32R, ffn_mem)
            ghi = sb("ghi", [P, FT, T], F32R, ffn_mem)
            glo = sb("glo", [P, FT, T], F32R, ffn_mem)
        with ExitStack() as y_mem:
            yT = sb("yT", [P, DT, T], F32, y_mem)
            with ExitStack() as out_mem:
                otok = sb("otok", [P, NT, D], F32, out_mem)
            xu_acc = sb("xu_acc", [P, T], F32, y_mem)
            uu_acc = sb("uu_acc", [P, T], F32, y_mem)
            xu_part = sb("xu_part", [P, T], F32, y_mem)
            uu_part = sb("uu_part", [P, 4, T], F32, y_mem)
            fb = sb("fb", [P, T], F32, y_mem)
        with l0_mem:
            sb("h_area0", [P, 2 * DT, T], F32, l0_mem)
            qkA = sb("qkA", [P, 6, T], F32, l0_mem)
            vA = sb("vA", [P, 3, NT, P], F32, l0_mem)
            qkB = sb("qkB", [P, 6, T], F32, l0_mem)
            vB = sb("vB", [P, 3, T], F32, l0_mem)
            prob = sb("prob", [P, 2, 6 * P], F32, l0_mem)
            probT = sb("probT", [P, 2, 6 * P], F32, l0_mem)
            osb = sb("osb", [P, NT, P], F32, l0_mem)
            ohi = sb("ohi", [P, PAIRS, T], F32R, l0_mem)
            olo = sb("olo", [P, PAIRS, T], F32R, l0_mem)
        with ExitStack() as start_mem:
            mstart = sb("mstart", [P, DT, DT, 2 * P], F32, start_mem)
            macc0 = sb("macc0", [P, 2 * DT, P], F32, start_mem)
            xtok = sb("xtok", [P, NT, D], F32, start_mem)
            rows = sb("rows", [P, 4, P], F32, start_mem)
            row1 = sb("row1", [1, 5, P], F32, start_mem)
            lamr = sb("lamr", [1, 4, HEAD_DIM], F32, start_mem)
            lams = sb("lams", [1, 8], F32, start_mem)
            posi = sb("posi", [P, T], I32, start_mem)
            ang = sb("ang", [P, 3, T], F32, start_mem)
        with l1_mem:
            sb("h_area1", [P, 2 * DT, T], F32, l1_mem)
            khi = sb("khi", [P, DT, T], F32R, l1_mem)
            klo = sb("klo", [P, DT, T], F32R, l1_mem)
            qkA1 = sb("qkA1", [P, 2, T], F32, l1_mem)
            vA1 = sb("vA1", [P, NT, P], F32, l1_mem)
            qkB1 = sb("qkB1", [P, 2, T], F32, l1_mem)
            vB1 = sb("vB1", [P, T], F32, l1_mem)
            prob1 = sb("prob1", [P, 2, T], F32, l1_mem)
            aprob = sb("aprob", [P, 2, T], F32, l1_mem)
            aprobT = sb("aprobT", [P, T], F32, l1_mem)
            osb1 = sb("osb1", [P, NT, P], F32, l1_mem)
            ohi1 = sb("ohi1", [P, HEADS_B, T], F32R, l1_mem)
            olo1 = sb("olo1", [P, HEADS_B, T], F32R, l1_mem)

        oraw = rb[:, 0:2 * P].rearrange("p (n d) -> p n d", n=2)

        def pb(name, shape):
            return ctx.enter_context(nc.psum_tensor(name, shape, F32))

        accs = pb("accs", [P, 3, T])
        acc = [accs[:, b, :] for b in range(3)]
        scores = pb("scores", [P, 2, T])

        def scores_of(s, proj):
            return scores[:] if proj or s % 2 == 0 else accs[:, 0:2, :]
        turned = [pb(f"turned{b}", [P, T]) for b in range(2)]
        pv_acc = pb("pv_acc", [P, T])

        def signal(name, stream, k=1, step=1, before=0):
            return Signal(nc, ctx, name, stream, k, step, before)

        w_landed = signal("w_landed", "chunk", 3, 16)
        hi_ready = signal("hi_ready", "chunk")
        lo_ready = signal("lo_ready", "chunk")
        chunk_used = signal("chunk_used", "chunk")
        acc_free = signal("acc_free", "bank", 3)
        t_ready = signal("t_ready", "tjob")
        t_free = signal("t_free", "tjob", 2)
        m_landed = signal("m_landed", "mod", 2, 16)
        m_scaled = signal("m_scaled", "mod")
        m_summed = signal("m_summed", "mod", before=2)
        s_ready = signal("s_ready", "unit")
        maxed = signal("maxed", "unit")
        exped = signal("exped", "unit", before=1)
        joined = signal("joined", "unit1")
        pv_ready = signal("pv_ready", "unit")
        o_out = signal("o_out", "unit", before=1)
        o_square = signal("o_square", "unit1")
        o_var = signal("o_var", "unit1")
        o_rms = signal("o_rms", "unit1")
        o_normed = signal("o_normed", "unit1")
        roped = signal("roped", "rope")
        b_to_a = signal("b_to_a", "turnover")
        sq_added = signal("sq_added", "ysq")
        y_squared = signal("y_squared", "ysq")
        xu_added = signal("xu_added", "xu")
        uu_added = signal("uu_added", "uu")
        gain_ready = signal("gain_ready", "gain")
        mean_ready = signal("mean_ready", "mean")
        stat_r = signal("stat_r", "stat")
        stat_d = signal("stat_d", "stat")
        y_scaled = signal("y_scaled", "yx")
        x_even = signal("x_even", "xe")
        x_odd = signal("x_odd", "xo")
        u_ready = signal("u_ready", "h")
        h_hi = signal("h_hi", "h")
        h_ready = signal("h_ready", "h")
        tap_ready = signal("tap_ready", "ff")
        gelu_ready = signal("gelu_ready", "ff")
        g_hi = signal("g_hi", "ff")
        g_ready = signal("g_ready", "ff", before=1)
        v_chain = signal("v_chain", "vchain")
        s_chain = signal("s_chain", "schain")
        g_chain = signal("g_chain", "gchain")
        x_landed = signal("x_landed", "x_landed", 1, 16)
        vec_landed = signal("vec_landed", "vec_landed", 1, 16)
        table_landed = signal("table_landed", "table_landed", 1, 16)
        row_landed = signal("row_landed", "row_landed", 1, 16)
        consts_ready = signal("consts_ready", "consts_ready")
        masks_ready = signal("masks_ready", "masks_ready")
        diffs_ready = signal("diffs_ready", "diffs_ready")
        near_ready = signal("near_ready", "near_ready")
        mods_landed = [signal(f"mods_landed{j}", f"mods_landed{j}", 1, 16) for j in range(DT)]
        rope_rows = signal("rope_rows", "rope_rows")
        c_exped = signal("c_exped", "c_exped")
        c_ready = signal("c_ready", "c_ready")
        lam_summed = signal("lam_summed", "lam_summed")
        lam_exped = signal("lam_exped", "lam_exped")
        lam_ready = signal("lam_ready", "lam_ready")
        angles_ready = signal("angles_ready", "angles_ready")
        sines_ready = signal("sines_ready", "sines_ready")
        tables_ready = signal("tables_ready", "tables_ready")
        x_squared = signal("x_squared", "x_squared")
        m0_scaled = signal("m0_scaled", "m0_scaled")
        m0_summed = signal("m0_summed", "m0_summed")
        out_ready = signal("out_ready", "otile", 2)
        stored = signal("stored", "stored", 1, 16)

        KINDS = [(g, w) for g in range(3) for w in (1, 0, 2)]
        A_TJOBS = 3 + 2 * 8 + 1
        VECS, TABLES, ROWS = 6, 7, 6
        PE_MODS, DVE_MODS = (0, 2, 5), (1, 3, 4, 6, 7)
        SHORT = (FT % DT) * P

        def tile_cols(j):
            return slice(j * P, (j + 1) * P)

        def by_class(ap):
            return ap.rearrange("p (i c) -> p c i", c=CLASSES)

        def classed(ap):
            return ap.rearrange("p (c i) -> p c i", c=CLASSES)

        def band_mask(cls):
            return band[:, (3 - cls) * P:(3 - cls) * P + T]

        block = ctx.enter_context(nc.Block())

        @block.sync
        def _(sp):
            at = Count(sp)

            def load(src, cols=P):
                sp.wait_ge(*at.done(lo_ready, -3))
                k = src.shape[1]
                dst = raw[:, at.at("chunk", 3), 0:k * cols].rearrange("p (k n) -> p k n", n=cols)
                sp.dma_start(dst, src).then_inc(*at.here(w_landed))
                at.passed("chunk")

            def columns(w, start, cols=P):
                return w[:, bass.ds(start, cols)].rearrange("(k p) n -> p k n", p=P)

            sp.dma_start(rows[C_ROW:C_ROW + DT, 0, :], c[0].rearrange("(r n) -> r n", n=P)).then_inc(*at.here(vec_landed))
            for dst, src in ((PRE_MIX, norm_pre_mix), (POST_MIX, norm_post_mix), (PRE_FFN, norm_pre_ffn), (POST_FFN, norm_post_ffn)):
                sp.dma_start(rows[dst:dst + 2 * DT, 0, :], src.rearrange("l (r n) -> (l r) n", n=P)).then_inc(*at.here(vec_landed))
            sp.dma_start(rows[KVN:KVN + DT, 0, :], kv_norm.rearrange("(r n) -> r n", n=P)).then_inc(*at.here(vec_landed))
            sp.dma_start(xtok[:], x[0].rearrange("(t p) d -> p t d", p=P)).then_inc(*at.here(x_landed))
            for j in range(DT):
                sp.dma_start(mstart[:, j], columns(mod_mix_w[0], 2 * P * j, 2 * P)).then_inc(mods_landed[j].sems[0], 16)

            def load_pair(start):
                for g, w in KINDS:
                    load(columns(a_w_qkv[0][:, (g * 3 + w) * A_INNER:(g * 3 + w + 1) * A_INNER], start))

            load_pair(0)
            with at.loop(PAIRS - 1, chunk=9) as turn:
                load_pair(turn * P + P)
            for q in range(DT // 2):
                load(columns(a_w_o[0], 2 * P * q, 2 * P), 2 * P)

            def load_ffn(layer):
                def gate_up(ft):
                    load(columns(ffn_w_gate[layer], ft * P))
                    load(columns(ffn_w_up[layer], ft * P))

                def down(dt):
                    for k0 in range(0, FT, DT):
                        k = min(DT, FT - k0)
                        rows_ = ffn_w_down[layer][k0 * P:(k0 + k) * P, :]
                        load(columns(rows_, dt * P))

                with at.loop(FT // FT_TURN, chunk=2 * FT_TURN) as turn:
                    for j in range(FT_TURN):
                        gate_up(turn * FT_TURN + j)
                gate_up(FT - 1)
                with at.loop(DT // 3, chunk=9) as turn:
                    for j in range(3):
                        down(turn * 3 + j)
                for dt in range(DT // 3 * 3, DT):
                    down(dt)

            load_ffn(0)

            def load_head(head):
                for w in (b_w_k, b_w_q[0], b_w_v):
                    load(columns(w, head * P))

            load_head(0)
            load_head(1)
            with at.loop(HEADS_B - 2, chunk=3) as turn:
                load_head(turn + 2)
            for dt in range(DT):
                load(columns(b_w_o[0], dt * P))
            load_ffn(1)

            for half in range(2):
                for t in range(NT):
                    sp.wait_ge(*at.done(out_ready))
                    sp.dma_start(out[0][t * P:(t + 1) * P, half * 512:half * 512 + 512],
                                 otok[:, t, half * 512:half * 512 + 512]).then_inc(*at.here(stored))
                    at.passed("otile")
                    at.passed("stored")
            sp.wait_ge(*at.done(stored, -1))

        @block.tensor
        def _(pe):
            at = Count(pe)

            def product(out_, w, rhs_hi, rhs_lo, first, last):
                slot, cols = w
                pe.matmul(out_, whi[:, slot, cols], rhs_hi, start=first, stop=False)
                pe.matmul(out_, whi[:, slot, cols], rhs_lo, start=False, stop=False)
                return pe.matmul(out_, wlo[:, slot, cols], rhs_hi, start=False, stop=last)

            def project(rhs, k0, k1, ksteps=DT, first=True, last=True, stride=P, col0=0, done=True, open_=True):
                bank = acc[at.at("bank", 3)]
                slot = at.at("chunk", 3)
                if open_:
                    if first:
                        pe.wait_ge(*at.done(acc_free, -3))
                    pe.wait_ge(*at.done(lo_ready))
                for k in range(k0, k1):
                    mm = product(bank[:], (slot, slice(k * stride + col0, k * stride + col0 + P)), rhs[0](k), rhs[1](k),
                                 first and k == 0, last and k == ksteps - 1)
                if done:
                    mm.then_inc(*at.here(chunk_used))
                    at.passed("chunk")
                    if last:
                        at.passed("bank")

            def keep_warm(n, bank=None):
                for _ in range(n):
                    pe.matmul((pv_acc if bank is None else bank)[:], identb[:], causal[:], start=True, stop=True)

            def project_first(chunks, finish=None):
                banks, slots = [], []
                for b in range(3):
                    pe.wait_ge(*at.done(acc_free, b - 3))
                    pe.wait_ge(*at.done(lo_ready, b))
                    banks.append(acc[(at.n.get("bank", 0) + b) % 3])
                    slots.append((at.n.get("chunk", 0) + b) % 3)

                def step(b, k, rhs):
                    return product(banks[b][:], (slots[b], slice(k * P, (k + 1) * P)), rhs[0](k), rhs[1](k), k == 0, k == DT - 1)

                for k in range(DT):
                    pe.wait_ge(*at.done(h_ready, k))
                    for b in range(3):
                        if finish is None or b == 0 or (b == 2 and k < DT - 1):
                            mm = step(b, k, chunks)
                            if k == DT - 1:
                                mm.then_inc(*at.here(chunk_used, b))
                at.passed("h", DT)
                if finish is not None:
                    for k in range(DT):
                        pe.wait_ge(*at.done(h_ready, k))
                        mm = step(1, k, finish)
                    mm.then_inc(*at.here(chunk_used, 1))
                    step(2, DT - 1, chunks).then_inc(*at.here(chunk_used, 2))
                    at.passed("h", DT)
                at.passed("chunk", 3)
                at.passed("bank", 3)

            def tiles(hi, lo, base=0):
                return (lambda k: hi[:, base + k, :]), (lambda k: lo[:, base + k, :])

            def job():
                pe.wait_ge(*at.done(t_free, -2))
                return turned[at.at("tjob", 2)]

            def job_done(ins):
                ins.then_inc(*at.here(t_ready))
                at.passed("tjob")

            def turn_tiles(srcs):
                bank = job()
                for j, s in enumerate(srcs):
                    ins = pe.transpose(bank[:, tile_cols(j)], s, identf[:])
                job_done(ins)

            def mod_columns(n0, n):
                pe.wait_ge(*at.done(m_summed, -1))
                bank = job()
                for j in range(n):
                    ins = pe.matmul(bank[:, j:j + 1], macc[:, n0 + j, :], onesf[:, 0:1], start=True, stop=True)
                job_done(ins)

            def token_sums(src, bank, col):
                for j in range(NT):
                    ins = pe.matmul(bank[:, col + j:col + j + 1], src[:, tile_cols(j)], onesf[:, 0:1], start=True, stop=True)
                return ins

            def spread_rms():
                pe.wait_ge(*at.done(stat_d))
                at.passed("stat")
                bank = job()
                job_done(pe.matmul(bank[:], onesf[:], tmp[:, 3, :], start=True, stop=True))

            def norm_stats(last=False):
                keep_warm(10)
                pe.wait_ge(*at.done(sq_added, DT - 1))
                at.passed("ysq", DT)
                job_done(token_sums(sqacc, job(), 0))
                if not last:
                    pe.wait_ge(*at.done(xu_added, DT - 1))
                    pe.wait_ge(*at.done(uu_added, DT - 1))
                    at.passed("xu", DT)
                    at.passed("uu", DT)
                    bank = job()
                    token_sums(xu_acc, bank, 0)
                    job_done(token_sums(uu_acc, bank, NT))
                    spread_rms()
                    keep_warm(8)
                spread_rms()
                if not last:
                    keep_warm(12)

            pe.wait_ge(*at.done(consts_ready))
            pe.wait_ge(*at.done(vec_landed, VECS - 1))

            def turn_rows(n, r):
                bank = job()
                job_done(pe.transpose(bank[:, 0:n], rows[0:n, r, :], identf[0:n, 0:n]))

            turn_rows(NVEC, 0)
            pe.wait_ge(*at.done(rope_rows))
            pe.wait_ge(*at.done(row_landed, ROWS - 1))
            bank = job()
            for j in range(5):
                ins = pe.matmul(bank[:, j:j + 1], row1[0:1, j, :], onesf[0:1, 0:1], start=True, stop=True)
            job_done(ins)
            pe.wait_ge(*at.done(x_landed))
            for k in range(DT):
                turn_tiles([xtok[:, t, tile_cols(k)] for t in range(NT)])
            pe.wait_ge(*at.done(c_ready))
            for j in PE_MODS:
                bank = job()
                pe.wait_ge(*at.done(mods_landed[j]))
                for half in range(2):
                    for k in range(DT):
                        ins = pe.matmul(bank[:, half:half + 1], mstart[:, j, k, tile_cols(half)], csil[:, k:k + 1],
                                        start=(k == 0), stop=(k == DT - 1))
                job_done(ins)
            pe.wait_ge(*at.done(table_landed, TABLES - 1))
            for n, r in ((NMOD, 1), (CONV, 2), (CONV, 3)):
                turn_rows(n, r)
            spread_rms()
            for j0, j1 in ((0, 3), (3, 5)):
                pe.wait_ge(*at.done(m0_summed, j1 - 1))
                bank = job()
                for j in range(j0, j1):
                    for half in range(2):
                        ins = pe.matmul(bank[:, 2 * (j - j0) + half:2 * (j - j0) + half + 1], macc0[:, 2 * DVE_MODS[j] + half, :],
                                        onesf[:, 0:1], start=True, stop=True)
                job_done(ins)
            pe.wait_ge(*at.done(lam_ready))
            bank = job()
            job_done(pe.matmul(bank[:, 0:1], onesf[0:1, :], lams[0:1, 4:5], start=True, stop=True))

            def pair_body(attend, proj):
                h = tiles(hhi, hlo)
                for s in range(10):
                    if proj and not attend and s == 0:
                        project_first(h)
                    elif attend and proj and s == 8:
                        project(h, 0, DT // 2, done=False)
                    elif proj and s < 9 and (attend or s > 2):
                        project(h, 0, DT)
                    if attend and s == 0:
                        for g in range(3):
                            if g == 0:
                                pe.wait_ge(*at.done(acc_free, -2 if proj else -1))
                            if g == 0 and not proj:
                                pe.wait_ge(*at.done(acc_free, -2))
                                pe.wait_ge(*at.done(acc_free, -3))
                            turn_tiles([vB[:, g, tile_cols(t)] for t in range(NT)])
                        pe.wait_ge(*at.done(b_to_a))
                        at.passed("turnover")
                    if attend and s < 8:
                        hh, cls = s // 4, s % 4
                        r = slice(hh * HEAD_DIM, (hh + 1) * HEAD_DIM)
                        sc = scores_of(s, proj)
                        pe.wait_ge(*at.done(exped, -1 if proj or s == 0 else -2))
                        pe.matmul(sc[:, 0, :], identb[:], band_mask(cls), start=True, stop=False)
                        pe.matmul(sc[:, 0, :], qkA[r, 0, tile_cols(cls)], qkA[r, 1, :], start=False, stop=True)
                        pe.matmul(sc[:, 1, 0:2 * P], identb[:], near[:], start=True, stop=False, skip_group_check=True)
                        for g in (1, 2):
                            mm = pe.matmul(sc[:, 1, tile_cols(g - 1)], qkA[r, 2 * g, tile_cols(cls)],
                                           qkA[r, 2 * g + 1, tile_cols(cls)], start=False, stop=(g == 2), skip_group_check=True)
                        mm.then_inc(*at.here(s_ready))
                        at.passed("unit")
                    if attend and not proj and s < 9:
                        keep_warm(2, acc[2])
                    if attend and 1 <= s <= 8:
                        u = (s - 1) % 2
                        pe.wait_ge(*at.done(exped, -2 if s < 8 else -1))
                        turn_tiles([prob[:, u, tile_cols(e)] for e in range(4)])
                        turn_tiles([prob[:, u, tile_cols(e)] for e in (4, 5)])
                    if attend and proj and s == 8:
                        project(h, DT // 2, DT, open_=False)
                    if attend and 2 <= s <= 9:
                        u, hh, cls = (s - 2) % 2, (s - 2) // 4, (s - 2) % 4
                        back = -4 if s <= 8 else -2
                        pe.wait_ge(*at.done(t_free, back))
                        pe.wait_ge(*at.done(t_free, back + 1))
                        unit = -3 if s < 8 else s - 10
                        pe.wait_ge(*at.done(o_out, unit - 1))
                        cols = slice(hh * HEAD_DIM, (hh + 1) * HEAD_DIM)
                        vs = [vA[:, 0, e, cols] for e in range(4)] + [vA[:, g, cls, cols] for g in (1, 2)]
                        for e, v in enumerate(vs):
                            mm = pe.matmul(pv_acc[:, 0:HEAD_DIM], probT[:, u, tile_cols(e)], v, start=(e == 0), stop=(e == 5))
                        mm.then_inc(*at.here(pv_ready, unit))
                if attend:
                    at.passed("mod", DT)
                    mod_columns(0, 4)
                    mod_columns(4, 4)
                if attend:
                    pe.wait_ge(*at.done(o_out, -1))
                    turn_tiles([osb[:, t, :] for t in range(NT)])

            pair_body(False, True)
            pe.wait_ge(*at.done(masks_ready))
            with at.loop(PAIRS - 1, chunk=9, bank=9, tjob=A_TJOBS + 2, unit=8, turnover=1, mod=DT):
                pair_body(True, True)
            pair_body(True, False)
            pe.wait_ge(*at.done(t_free, -1))
            for q in range(DT // 2):
                project(tiles(ohi, olo), 0, PAIRS, PAIRS, stride=2 * P, done=False)
                at.passed("bank")
                pe.wait_ge(*at.done(acc_free, -3))
                project(tiles(ohi, olo), 0, PAIRS, PAIRS, stride=2 * P, col0=P, open_=False)
            norm_stats()

            def ffn(mods):
                h = tiles(hhi, hlo)

                def down(first):
                    for k0 in range(0, FT, DT):
                        k = min(DT, FT - k0)
                        if first:
                            pe.wait_ge(*at.done(g_ready, k0 + k - 1))
                        project(tiles(ghi, glo, k0), 0, k, k, first=(k0 == 0), last=(k0 + k == FT))

                def turn_mods(n):
                    at.passed("mod", n)
                    mod_columns(0, n // 2)
                    mod_columns(n // 2, n // 2)

                project_first(h)
                for j in range(3):
                    project(h, 0, DT)
                if mods:
                    turn_mods(4)
                with at.loop(MOD_TURNS - 1, chunk=6, bank=6, **(dict(mod=4, tjob=2) if mods else {})):
                    for j in range(6):
                        project(h, 0, DT)
                    if mods:
                        turn_mods(4)
                for j in range(2 * (FT - MOD_TURNS * FT_TURN)):
                    project(h, 0, DT)
                loop_counts = dict(chunk=9, bank=3) | (dict(mod=6, tjob=2) if mods else {})
                with at.loop(DT // 3, **loop_counts):
                    for j in range(3):
                        down(j == 0)
                    if mods:
                        turn_mods(6)
                if not mods:
                    turn_mods(8)
                for j in range(DT % 3):
                    down(False)
                at.passed("ff", FT)
                if mods:
                    turn_mods(4)
                norm_stats(last=not mods)

            ffn(True)

            def head_body(attend, proj, back):
                hk, hq = tiles(khi, klo), tiles(hhi, hlo)
                units = 0
                for s in range(7):
                    if proj and not attend and s == 0:
                        project_first(hk, hq)
                    elif proj and attend and s < 6:
                        m, half = s // 2, s % 2
                        if s < 5:
                            project(hq if m == 1 else hk, half * 4, half * 4 + 4, open_=(half == 0), done=(half == 1))
                    if attend and s == 0:
                        pe.wait_ge(*at.done(acc_free, -1))
                        if not proj:
                            pe.wait_ge(*at.done(acc_free, -2))
                            pe.wait_ge(*at.done(acc_free, -3))
                        turn_tiles([vB1[:, tile_cols(t)] for t in range(NT)])
                    if back and s == 1:
                        pe.wait_ge(*at.done(o_normed, -1 - units))
                        turn_tiles([osb1[:, t, :] for t in range(NT)])
                    if attend and s == 0:
                        pe.wait_ge(*at.done(b_to_a))
                        at.passed("turnover")
                    if attend and s < 4:
                        n = s
                        L = (n + 1) * P
                        sc = scores_of(s, proj)
                        pe.wait_ge(*at.done(exped, -1 if proj or s == 0 else -2))
                        for comp in range(2):
                            r = slice(comp * HEAD_DIM, (comp + 1) * HEAD_DIM)
                            pe.matmul(sc[:, comp, 0:L], identb[:], causal[:, (3 - n) * P:T], start=True, stop=False)
                            mm = pe.matmul(sc[:, comp, 0:L], qkA1[r, 0, tile_cols(n)], qkA1[r, 1, 0:L], start=False, stop=True)
                        mm.then_inc(*at.here(s_ready))
                        at.passed("unit")
                        at.passed("unit1")
                        units += 1
                    if attend and not proj:
                        keep_warm(1, acc[2])
                    if attend and 2 <= s <= 5:
                        n = s - 2
                        pe.wait_ge(*at.done(joined, n - units))
                        turn_tiles([aprob[:, n % 2, tile_cols(e)] for e in range(n + 1)])
                    if attend and 3 <= s <= 6:
                        n = s - 3
                        pe.wait_ge(*at.done(t_free, -2 if s < 6 else -1))
                        pe.wait_ge(*at.done(o_out, n - units - 1))
                        for e in range(n + 1):
                            mm = pe.matmul(pv_acc[:, 0:P], aprobT[:, tile_cols(e)], vA1[:, e, :], start=(e == 0), stop=(e == n))
                        mm.then_inc(*at.here(pv_ready, n - units))
                    if proj and attend and s == 5:
                        project(hk, 4, 8, open_=False)
                if attend:
                    at.passed("mod", 2)
                    mod_columns(0, 1)
                    mod_columns(1, 1)

            head_body(False, True, False)
            head_body(True, True, False)
            with at.loop(HEADS_B - 2, chunk=3, bank=3, tjob=8, unit=4, unit1=4, turnover=1, mod=2):
                head_body(True, True, True)
            head_body(True, False, True)
            pe.wait_ge(*at.done(o_normed, -1))
            turn_tiles([osb1[:, t, :] for t in range(NT)])
            pe.wait_ge(*at.done(t_free, -1))
            for dt in range(DT):
                project(tiles(ohi1, olo1), 0, DT)
            norm_stats()
            ffn(False)

            at.passed("xe", 3 * DT // 2)
            at.passed("xo", 3 * DT // 2)
            for half in range(2):
                for t in range(NT):
                    for j in range(4 if t == 0 else 0):
                        k = half * 4 + j
                        pe.wait_ge(*at.done((x_odd if k % 2 else x_even), 0))
                        at.passed("xo" if k % 2 else "xe")
                    if half * NT + t >= 2:
                        pe.wait_ge(*at.done(out_ready, -2))
                        bank = turned[at.at("tjob", 2)]
                    else:
                        bank = job()
                    for j in range(4):
                        ins = pe.transpose(bank[:, tile_cols(j)], xT[:, half * 4 + j, tile_cols(t)], identf[:])
                    job_done(ins)
                    at.passed("otile")

        @block.scalar
        def _(act):
            at = Count(act)

            def split_head(ahead=2, size=1024):
                slot = (at.n.get("chunk", 0) + ahead) % 3
                act.wait_ge(*at.done(w_landed, ahead))
                act.wait_ge(*at.done(chunk_used, ahead - 3))
                act.activation(whi[:, slot, 0:size], raw[:, slot, 0:size], ACT.Copy).then_inc(*at.here(hi_ready, ahead))

            def job_ready():
                act.wait_ge(*at.done(t_ready))
                return turned[at.at("tjob", 2)]

            def job_read(ins):
                ins.then_inc(*at.here(t_free))
                at.passed("tjob")

            def spread_rms():
                at.passed("tjob")
                bank = job_ready()
                job_read(act.activation(rb[:], bank[:], ACT.Copy))

            def read_y(dt, slot, post=None):
                bank = acc[at.at("bank", 3)]
                act.wait_ge(*at.done(chunk_used, 0))
                act.wait_ge(*at.done(sq_added, -3))
                act.activation(tmp[:, slot, :], bank[:], ACT.Square).then_inc(*at.here(y_squared))
                if post is None:
                    act.activation(yT[:, dt, :], bank[:], ACT.Copy).then_inc(*at.here(acc_free))
                else:
                    act.wait_ge(*at.done(uu_added, -3))
                    gain = postg[:, bass.ds(dt + post * DT, 1)]
                    act.activation(yT[:, dt, :], bank[:], ACT.Identity, scale=gain).then_inc(*at.here(s_chain))
                    at.passed("schain")
                    act.activation(uu_part[:, slot, :], bank[:], ACT.Square, scale=gain).then_inc(*at.here(acc_free))
                    at.passed("uu")
                at.passed("bank")
                at.passed("ysq")

            def heads_of_h(dst, shift):
                for k in range(DT):
                    act.wait_ge(*at.done(u_ready))
                    act.activation(dst[:, k, :], tmp[:, at.at("h", 3), :], ACT.Identity,
                                   bias=modc[:, shift + k:shift + k + 1]).then_inc(*at.here(h_hi))
                    at.passed("h")

            for j, v in enumerate((b_lambda_q1, b_lambda_q2, b_lambda_k1, b_lambda_k2)):
                act.dma_start(lamr[0:1, j, :], v).then_inc(*at.here(row_landed))
            act.dma_start(row1[0:1, 4, :], b_subln).then_inc(*at.here(row_landed))
            act.dma_start(posi[:], positions.to_broadcast([P, T])).then_inc(*at.here(row_landed))
            act.dma_start(rows[0:6 * DT, 1, :], mod_mix_b.rearrange("l (r n) -> (l r) n", n=P)).then_inc(*at.here(table_landed))
            act.dma_start(rows[6 * DT:12 * DT, 1, :], mod_ffn_b.rearrange("l (r n) -> (l r) n", n=P)).then_inc(*at.here(table_landed))
            act.dma_start(rows[12 * DT:14 * DT, 1, :], kv_mod_b.rearrange("(r n) -> r n", n=P)).then_inc(*at.here(table_landed))
            for layer in range(2):
                act.dma_start(rows[0:3 * FT, 2 + layer, :], ffn_conv_w[layer].rearrange("w (r n) -> (w r) n", n=P)).then_inc(*at.here(table_landed))
                act.dma_start(rows[3 * FT:4 * FT, 2 + layer, :], ffn_conv_b[layer].rearrange("(r n) -> r n", n=P)).then_inc(*at.here(table_landed))

            act.wait_ge(*at.done(t_free))
            act.activation(EXPC, vcol[:, C_ROW:C_ROW + DT], ACT.Exp, scale=-1.0).then_inc(*at.here(c_exped))
            act.wait_ge(*at.done(lam_summed))
            act.activation(lams[0:1, 2:4], lams[0:1, 0:2], ACT.Exp).then_inc(*at.here(lam_exped))
            at.passed("tjob", 2)
            for k in range(DT):
                bank = job_ready()
                job_read(act.activation(xT[:, k, :], bank[:], ACT.Copy))
            act.wait_ge(*at.done(x_landed))
            for t in range(NT):
                act.activation(tmp[:, 0:2, :].rearrange("p a n -> p (a n)"), xtok[:, t, :], ACT.Square,
                               accum_out=STAT_V[:, t:t + 1]).then_inc(*at.here(x_squared))
                act.wait_ge(*at.done(x_squared))
                at.passed("x_squared")
            act.wait_ge(*at.done(angles_ready))
            for dst, j in ((sinT, 0), (cosT, 1)):
                act.activation(dst[:], ang[:, j, :], ACT.Sin).then_inc(*at.here(sines_ready))
                at.passed("sines_ready")
            split_head(0)
            split_head(1)
            split_head(2)
            at.passed("tjob", 3 + len(PE_MODS))
            bank = job_ready()
            job_read(act.activation(rb[:], bank[:], ACT.Copy))
            at.passed("tjob", 3)
            act.wait_ge(*at.done(t_free, -1))
            heads_of_h(hhi, MIX[0])

            def read_head_of_o(dst, natural, scale=None):
                bank = job_ready()
                src = classed(bank[:]) if natural is not None else bank[:]
                func = dict(func=ACT.Copy) if scale is None else dict(func=ACT.Copy, scale=scale)
                act.activation(dst, src, **func).then_inc(*at.here(s_chain))
                at.passed("schain")
                at.passed("tjob")

            def pair_body(attend, proj, pair):
                def read_v(s):
                    if s % 3 == 2:
                        act.wait_ge(*at.done(chunk_used))
                        act.activation(vB[:, s // 3, :], acc[at.at("bank", 3)][:], ACT.Copy).then_inc(*at.here(acc_free))
                    at.passed("chunk")
                    at.passed("bank")

                for s in range(10):
                    if proj and s < (8 if attend else 9):
                        read_v(s)
                        if not attend:
                            split_head()
                    if attend and s == 0:
                        for g in range(3):
                            bank = job_ready()
                            job_read(act.activation(vA[:, g].rearrange("p t n -> p (t n)"), bank[:], ACT.Copy))
                    if attend and s < 8:
                        u = s % 2
                        act.wait_ge(*at.done(maxed))
                        act.activation(prob[:, u, :], scores_of(s, proj).rearrange("p b n -> p (b n)")[:, 0:6 * P], ACT.Exp,
                                       bias=nmax[:, u, 0:1], accum_out=den[:, s % 4, 0:1]).then_inc(*at.here(exped))
                        at.passed("unit")
                    if attend and 1 <= s <= 8:
                        u = (s - 1) % 2
                        for c0, c1 in ((0, 4 * P), (4 * P, 6 * P)):
                            bank = job_ready()
                            job_read(act.activation(probT[:, u, c0:c1], bank[:, 0:c1 - c0], ACT.Copy))
                    if attend and proj and s == 8:
                        read_v(s)
                    if attend and proj and s < 9:
                        split_head()
                if attend:
                    at.passed("tjob", 2)
                    dst = ohi[:, bass.ds(pair, 1), :].rearrange("p a (i c) -> p (a c) i", c=CLASSES)
                    read_head_of_o(dst, True)

            act.preload_act_table(ACT.Exp)
            pair_body(False, True, 0)
            with at.loop(PAIRS - 1, chunk=9, bank=9, tjob=A_TJOBS + 2, unit=8, schain=1) as turn:
                pair_body(True, True, turn)
            pair_body(True, False, PAIRS - 1)

            def transition(shifts):
                at.passed("tjob", 2)
                for dst in (fb, rb):
                    bank = job_ready()
                    job_read(act.activation(dst[:], bank[:], ACT.Copy))
                for dst, shift in shifts:
                    heads_of_h(dst, shift)

            act.wait_ge(*at.done(gain_ready))
            at.passed("gain")
            for q in range(DT // 2):
                read_y(2 * q, (2 * q) % 3, 0)
                read_y(2 * q + 1, (2 * q + 1) % 3, 0)
                at.passed("chunk")
                split_head()
            act.preload_act_table(ACT.Gelu_apprx_tanh)
            transition([(hhi, FFN[0])])

            def ffn(layer, mods, end):
                def feature_tile(ft, size=1024):
                    base = layer * CONV
                    act.wait_ge(*at.done(chunk_used))
                    act.activation(tmp[:, 0, :], acc[at.at("bank", 3)][:], ACT.Identity,
                                   bias=convc[:, bass.ds(ft + (base + 3 * FT), 1)],
                                   scale=convc[:, bass.ds(ft + (base + 2 * FT), 1)]).then_inc(*at.here(tap_ready))
                    at.passed("chunk")
                    split_head()
                    act.wait_ge(*at.done(acc_free))
                    act.activation(tmp[:, 1, :], tmp[:, 0, :], ACT.Gelu_apprx_tanh).then_inc(*at.here(gelu_ready))
                    act.wait_ge(*at.done(acc_free, 1))
                    act.activation(ghi[:, bass.ds(ft, 1), :].rearrange("p a n -> p (a n)"), tmp[:, 2, :], ACT.Copy).then_inc(*at.here(g_hi))
                    at.passed("chunk")
                    split_head(size=size)
                    at.passed("bank", 2)
                    at.passed("ff")

                with at.loop(MOD_TURNS, chunk=6, bank=6, ff=3, **(dict(tjob=2) if mods else {})) as turn:
                    for j in range(FT_TURN):
                        feature_tile(turn * FT_TURN + j)
                    if mods:
                        at.passed("tjob", 2)
                for ft in range(MOD_TURNS * FT_TURN, FT):
                    feature_tile(ft, 1024 if ft < FT - 1 else SHORT)

                def down(dt, slot, last=False):
                    for j in range(3):
                        if j == 2:
                            read_y(dt, slot, None if end else 1)
                        at.passed("chunk")
                        if not (last and end):
                            split_head(size=SHORT if j == 2 and not last else 1024)

                counts = dict(chunk=9, bank=3, ysq=3) | (dict(tjob=2) if mods else {}) | ({} if end else dict(schain=3, uu=3))
                with at.loop(DT // 3, **counts) as turn:
                    for j in range(3):
                        down(turn * 3 + j, j)
                    if mods:
                        at.passed("tjob", 2)
                for dt in range(DT // 3 * 3, DT):
                    down(dt, dt % 3, dt == DT - 1)
                at.passed("tjob", 2)

            ffn(0, True, False)
            act.preload_act_table(ACT.Exp)
            transition([(khi, KV), (hhi, MIX[1])])

            def head_body(attend, proj, back, head):
                units = 0
                def read_v():
                    act.wait_ge(*at.done(chunk_used))
                    act.activation(vB1[:], acc[at.at("bank", 3)][:], ACT.Copy).then_inc(*at.here(acc_free))

                for s in range(7):
                    if attend and s == 0:
                        bank = job_ready()
                        job_read(act.activation(vA1[:].rearrange("p t n -> p (t n)"), bank[:], ACT.Copy))
                    if back and s == 1:
                        read_head_of_o(ohi1[:, bass.ds(head, 1), :].rearrange("p a n -> p (a n)"), None, small[:, SUBG:SUBG + 1])
                    if attend and s < 4:
                        n, u = s, s % 2
                        L = (n + 1) * P
                        act.wait_ge(*at.done(maxed))
                        act.wait_ge(*at.done(joined, -1))
                        for comp in range(2):
                            ins = act.activation(prob1[:, comp, 0:L], scores_of(s, proj)[:, comp, 0:L], ACT.Exp,
                                                 bias=nmax[:, u, comp:comp + 1], accum_out=den[:, n, comp:comp + 1])
                        ins.then_inc(*at.here(exped))
                        at.passed("unit")
                        at.passed("unit1")
                        units += 1
                    if attend and 2 <= s <= 5:
                        n = s - 2
                        bank = job_ready()
                        act.wait_ge(*at.done(pv_ready, n - units - 1))
                        job_read(act.activation(aprobT[:, 0:(n + 1) * P], bank[:, 0:(n + 1) * P], ACT.Copy))
                    if attend and 3 <= s <= 6:
                        n = s - 3
                        act.wait_ge(*at.done(pv_ready, n - units))
                        act.wait_ge(*at.done(o_normed, n - units - 2))
                        act.activation(oraw[:, n % 2, :], pv_acc[:, 0:P], ACT.Copy).then_inc(*at.here(o_out, n - units))
                        act.wait_ge(*at.done(o_out, n - units))
                        act.activation(tmp[:, 3, 0:P], oraw[:, n % 2, :], ACT.Square,
                                       accum_out=small[:, 24 + n % 2:25 + n % 2]).then_inc(*at.here(o_square, n - units))
                    if proj and s in (1, 3, 5):
                        if s == 5:
                            read_v()
                        at.passed("chunk")
                        at.passed("bank")
                        split_head()
                if attend:
                    at.passed("tjob", 2)

            head_body(False, True, False, 0)
            head_body(True, True, False, 0)
            with at.loop(HEADS_B - 2, chunk=3, bank=3, tjob=8, unit=4, unit1=4, schain=1) as turn:
                head_body(True, True, True, turn)
            head_body(True, False, True, HEADS_B - 2)
            read_head_of_o(ohi1[:, HEADS_B - 1, :], None, small[:, SUBG:SUBG + 1])
            act.wait_ge(*at.done(gain_ready))
            at.passed("gain")
            for dt in range(DT):
                read_y(dt, dt % 3, 2)
                at.passed("chunk")
                split_head()
            act.preload_act_table(ACT.Gelu_apprx_tanh)
            transition([(hhi, FFN[1])])
            ffn(1, False, True)
            spread_rms()
            for j in range(8):
                half, t = j // 4, j % 4
                if j % 2:
                    bank = job_ready()
                    act.activation(otok[:, t, half * 512:half * 512 + 512], bank[:], ACT.Copy).then_inc(*at.here(out_ready))
                at.passed("otile")
                at.passed("tjob")

        @block.vector
        def _(dve):
            at = Count(dve)

            def chain(ins):
                ins.then_inc(*at.here(v_chain))
                dve.wait_ge(*at.done(v_chain))
                at.passed("vchain")

            def split_rest(ahead=2, size=1024):
                slot = (at.n.get("chunk", 0) + ahead) % 3
                dve.wait_ge(*at.done(hi_ready, ahead))
                head = whi[:, slot, 0:size].bitcast(F32)
                dve.tensor_tensor(wlo[:, slot, 0:size], raw[:, slot, 0:size], head, ALU.subtract).then_inc(*at.here(lo_ready, ahead))

            def job_ready():
                dve.wait_ge(*at.done(t_ready))
                return turned[at.at("tjob", 2)]

            def job_read(ins):
                ins.then_inc(*at.here(t_free))
                at.passed("tjob")

            def factors():
                bank = job_ready()
                job_read(dve.tensor_scalar(STAT_V, bank[:, 0:NT], 1.0 / D, NORM_EPS, ALU.mult, ALU.add))
                diagonal(STAT_R)
                dve.wait_ge(*at.done(t_free))
                at.passed("tjob")

            def diagonal(factors_):
                dve.wait_ge(*at.done(stat_r))
                dve.tensor_tensor(tmp[:, 3, :].rearrange("p (a b) -> p a b", a=NT),
                                  identf[:].rearrange("p (a b) -> p a b", a=1).to_broadcast([P, NT, P]),
                                  factors_.rearrange("p (a b) -> p a b", b=1).to_broadcast([P, NT, P]),
                                  ALU.mult).then_inc(*at.here(stat_d))
                at.passed("stat")

            def updated(k):
                dve.tensor_tensor(yT[:, k, :], yT[:, k, :], fb[:], ALU.mult).then_inc(*at.here(v_chain))
                dve.wait_ge(*at.done(v_chain))
                at.passed("vchain")
                dve.tensor_tensor(xT[:, k, :], xT[:, k, :], yT[:, k, :], ALU.add).then_inc(*at.here(x_even, k // 2))

            def norms():
                bank = job_ready()
                job_read(dve.tensor_scalar(STAT_V, bank[:, 0:NT], 1.0 / D, NORM_EPS, ALU.mult, ALU.add))
                diagonal(STAT_R)
                bank = job_ready()
                chain(dve.tensor_tensor(GAIN_X, bank[:, NT:2 * NT], STAT_R, ALU.mult))
                job_read(dve.scalar_tensor_tensor(GAIN_X, bank[:, 0:NT], 2.0, GAIN_X, ALU.mult, ALU.add))
                dve.wait_ge(*at.done(t_free, -1))
                chain(dve.scalar_tensor_tensor(GAIN_X, GAIN_X, 1.0 / D, STAT_R, ALU.mult, ALU.mult))
                chain(dve.tensor_tensor(MEAN_X, MEAN_X, GAIN_X, ALU.add))
                chain(dve.tensor_scalar(MEAN_X, MEAN_X, 0.0, None, ALU.max))
                dve.tensor_scalar(STAT_V, MEAN_X, NORM_EPS, None, ALU.add).then_inc(*at.here(mean_ready))
                at.passed("mean")
                dve.wait_ge(*at.done(t_free))
                at.passed("tjob")
                updated(0)
                diagonal(STAT_Q)
                updated(2)
                dve.wait_ge(*at.done(t_free))
                at.passed("tjob")

            def update_x(post):
                for k in range(DT):
                    dve.scalar_tensor_tensor(yT[:, k, :], yT[:, k, :], postg[:, post * DT + k:post * DT + k + 1], rb[:],
                                             ALU.mult, ALU.mult).then_inc(*at.here(y_scaled))
                    if k % 2 == 0:
                        dve.wait_ge(*at.done(y_scaled))
                        dve.tensor_tensor(xT[:, k, :], xT[:, k, :], yT[:, k, :], ALU.add).then_inc(*at.here(x_even))
                        at.passed("xe")
                    else:
                        at.passed("xo")
                    at.passed("yx")

            def normed(hi, lo, pre, shift, classes=False, update=False):
                def scaled(k):
                    order = by_class if classes else (lambda a: a)
                    dst = classed(tmp[:, at.at("h", 3), :]) if classes else tmp[:, at.at("h", 3), :]
                    dve.wait_ge(*at.done(h_ready, -3))
                    if update:
                        dve.wait_ge(*at.done(x_odd if k % 2 else x_even, k // 2))
                    dve.scalar_tensor_tensor(dst, order(xT[:, k, :]), presc[:, pre * DT + k:pre * DT + k + 1], order(rb[:]),
                                             ALU.mult, ALU.mult).then_inc(*at.here(u_ready))
                    at.passed("h")

                def rest(k, back):
                    dve.wait_ge(*at.done(h_hi, -back))
                    slot = (at.n["h"] - back) % 3
                    dve.scalar_tensor_tensor(lo[:, k, :], tmp[:, slot, :], modc[:, shift + k:shift + k + 1],
                                             hi[:, k, :].bitcast(F32), ALU.add, ALU.subtract).then_inc(*at.here(h_ready, -back))

                scaled(0)
                for k in range(DT):
                    if update and k + 3 in (4, 6):
                        updated(k + 3)
                    if k + 1 < DT:
                        scaled(k + 1)
                    rest(k, 2 if k + 1 < DT else 1)
                if update:
                    at.passed("xe", DT // 2)
                    at.passed("xo", DT // 2)

            def mod_columns(col, n):
                bank = job_ready()
                job_read(dve.tensor_tensor(modc[:, bass.ds(col, n)], bank[:, 0:n], bcol[:, bass.ds(col, n)], ALU.add))

            def mod_sum(j):
                dve.wait_ge(*at.done(m_scaled))
                dve.tensor_reduce(macc[:, j, :], mraw[:, at.at("mod", 2)].rearrange("p k n -> p n k"), AX.X, ALU.add).then_inc(*at.here(m_summed))
                at.passed("mod")

            def pre_scale(set_, col, gain):
                chain(dve.scalar_tensor_tensor(presc[:, set_ * DT:(set_ + 1) * DT], modc[:, col + DT:col + 2 * DT], 1.0,
                                               vcol[:, gain:gain + DT], ALU.add, ALU.mult))

            def post_gain(set_, col, gain):
                chain(dve.tensor_tensor(postg[:, set_ * DT:(set_ + 1) * DT], modc[:, col + 2 * DT:col + 3 * DT],
                                        vcol[:, gain:gain + DT], ALU.mult))

            dve.wait_ge(*at.done(consts_ready))
            for col, sig in enumerate((exped, o_out, g_ready, m_summed, m_summed)):
                dve.memset(marks[:, col:col + 1], 0.0).then_inc(*at.here(sig))
            chain(dve.tensor_copy(identb[:], identf[:]))
            rope = row1[0:1, 0:4, :].rearrange("o r (h d) -> o r h d", d=HEAD_DIM)
            chain(dve.memset(row1[0:1, 0:4, :], 0.0))
            for f in range(ROT_HALF):
                inv = float(np.float32(ROPE_THETA ** (-f / ROT_HALF)))
                for half in range(2):
                    chain(dve.memset(rope[:, 0, :, f + half * ROT_HALF:f + half * ROT_HALF + 1], inv))
            chain(dve.memset(rope[:, 1, :, 0:2 * ROT_HALF], 1.0))
            chain(dve.memset(rope[:, 2, :, 2 * ROT_HALF:HEAD_DIM], 1.0))
            chain(dve.memset(rope[:, 3, :, 0:ROT_HALF], -1.0))
            dve.memset(rope[:, 3, :, ROT_HALF:2 * ROT_HALF], 1.0).then_inc(*at.here(rope_rows))
            dve.wait_ge(*at.done(row_landed, ROWS - 1))
            chain(dve.tensor_tensor(lamr[0:1, 0:2, :], lamr[0:1, 0:2, :], lamr[0:1, 2:4, :], ALU.mult))
            dve.tensor_reduce(lams[0:1, 0:2], lamr[0:1, 0:2, :], AX.X, ALU.add).then_inc(*at.here(lam_summed))
            def read_columns(dst, n):
                bank = job_ready()
                job_read(dve.tensor_copy(dst, bank[:, 0:n]))

            read_columns(vcol[:], NVEC)
            read_columns(small[:, 0:5], 5)
            dve.wait_ge(*at.done(c_exped))
            chain(dve.tensor_scalar(EXPC, EXPC, 1.0, None, ALU.add))
            chain(dve.reciprocal(EXPC, EXPC))
            dve.tensor_tensor(csil[:], vcol[:, C_ROW:C_ROW + DT], EXPC, ALU.mult).then_inc(*at.here(c_ready))
            dve.wait_ge(*at.done(lam_exped))
            chain(dve.tensor_tensor(lams[0:1, 5:6], lams[0:1, 3:4], lams[0:1, 2:3], ALU.subtract))
            dve.tensor_scalar(lams[0:1, 4:5], lams[0:1, 5:6], -LAM_INIT, None, ALU.add).then_inc(*at.here(lam_ready))
            dve.wait_ge(*at.done(t_free, -1))
            chain(dve.tensor_scalar(small[:, SUBG:SUBG + 1], small[:, SUBLN:SUBLN + 1], 1.0 - LAM_INIT, None, ALU.mult))
            a0, a1, k0 = ang[:, 0, :], ang[:, 1, :], ang[:, 2, :]
            two_pi = 2.0 * math.pi
            part1 = 6.28125
            part2 = math.floor((two_pi - part1) * 2 ** 20) / 2 ** 20
            part3 = two_pi - part1 - part2
            rounder = 1.5 * 2 ** 23
            limit = 3.1415925
            chain(dve.tensor_copy(k0, posi[:]))
            chain(dve.tensor_scalar(a0, k0, small[:, FREQ:FREQ + 1], None, ALU.mult))
            chain(dve.tensor_scalar(k0, a0, 1.0 / two_pi, rounder, ALU.mult, ALU.add))
            chain(dve.tensor_scalar(k0, k0, -rounder, None, ALU.add))
            for part in (part1, part2, part3):
                chain(dve.scalar_tensor_tensor(a0, k0, -part, a0, ALU.mult, ALU.add))
            chain(dve.tensor_scalar(a1, a0, math.pi / 2, None, ALU.add))
            chain(dve.tensor_scalar(k0, a1, limit, -two_pi, ALU.is_gt, ALU.mult))
            chain(dve.tensor_tensor(a1, a1, k0, ALU.add))
            dve.tensor_scalar(ang[:, 0:2, :], ang[:, 0:2, :], limit, -limit, ALU.min, ALU.max).then_inc(*at.here(angles_ready))
            dve.wait_ge(*at.done(diffs_ready))
            diffs = tmp[:, 3, 0:P].bitcast(I32)
            chain(dve.tensor_single_scalar(diffs, diffs, 3, ALU.bitwise_and))
            dve.tensor_scalar(near[:, P:2 * P], diffs, 0.0, MASKED, ALU.is_gt, ALU.mult).then_inc(*at.here(near_ready))

            at.passed("tjob", DT)

            def first_mods(j):
                dve.wait_ge(*at.done(mods_landed[j]))
                odd = mstart[:, j, :, P:2 * P]
                chain(dve.tensor_tensor(odd, odd, csil[:].rearrange("p (k a) -> p k a", a=1).to_broadcast([P, DT, P]), ALU.mult))
                chain(dve.tensor_reduce(macc0[:, 2 * j + 1, :], odd.rearrange("p k n -> p n k"), AX.X, ALU.add))
                dve.wait_ge(*at.done(m0_scaled))
                at.passed("m0_scaled")
                dve.tensor_reduce(macc0[:, 2 * j, :], mstart[:, j, :, 0:P].rearrange("p k n -> p n k"), AX.X, ALU.add).then_inc(*at.here(m0_summed))
                at.passed("m0_summed")

            first_mods(DVE_MODS[0])
            dve.wait_ge(*at.done(x_squared, NT - 1))
            chain(dve.tensor_scalar(MEAN_X, STAT_V, 1.0 / D, None, ALU.mult))
            dve.tensor_scalar(STAT_V, MEAN_X, NORM_EPS, None, ALU.add).then_inc(*at.here(mean_ready))
            at.passed("mean")
            first_mods(DVE_MODS[1])
            read_columns(modc[:, 2 * PE_MODS[0]:2 * PE_MODS[0] + 2], 2)
            diagonal(STAT_R)
            first_mods(DVE_MODS[2])
            first_mods(DVE_MODS[3])
            read_columns(modc[:, 2 * PE_MODS[1]:2 * PE_MODS[1] + 2], 2)
            first_mods(DVE_MODS[4])
            read_columns(modc[:, 2 * PE_MODS[2]:2 * PE_MODS[2] + 2], 2)
            for dst, n in ((bcol[:], NMOD), (convc[:, 0:CONV], CONV), (convc[:, CONV:2 * CONV], CONV)):
                read_columns(dst, n)
            dve.wait_ge(*at.done(t_free, -1))
            for j in PE_MODS:
                ins = dve.tensor_tensor(modc[:, 2 * j:2 * j + 2], modc[:, 2 * j:2 * j + 2], bcol[:, 2 * j:2 * j + 2], ALU.add)
            for chunk in range(3):
                split_rest(chunk)
            dve.wait_ge(*at.done(t_free))
            at.passed("tjob")
            for pairs in (DVE_MODS[0:3], DVE_MODS[3:5]):
                bank = job_ready()
                for n, j in enumerate(pairs):
                    ins = dve.tensor_tensor(modc[:, 2 * j:2 * j + 2], bank[:, 2 * n:2 * n + 2], bcol[:, 2 * j:2 * j + 2], ALU.add)
                job_read(ins)
            bank = job_ready()
            job_read(dve.tensor_copy(small[:, NEGLAM:NEGLAM + 1], bank[:, 0:1]))
            dve.wait_ge(*at.done(t_free, -1))
            dve.wait_ge(*at.done(t_free, -2))
            pre_scale(0, MIX[0], PRE_MIX)
            normed(hhi, hlo, 0, MIX[0], classes=True)
            dve.wait_ge(*at.done(sines_ready, 1))
            chain(dve.tensor_scalar(sinT[:], sinT[:], small[:, RSIGN:RSIGN + 1], None, ALU.mult))
            dve.tensor_scalar(cosT[:], cosT[:], small[:, RMASK:RMASK + 1], small[:, RKEEP:RKEEP + 1], ALU.mult, ALU.add).then_inc(*at.here(tables_ready))
            dve.wait_ge(*at.done(tables_ready))

            partner = [(i + ROT_HALF) % (2 * ROT_HALF) if i < 2 * ROT_HALF else i for i in range(32)]

            def rope_read(classes):
                bank = acc[at.at("bank", 3)]
                dve.wait_ge(*at.done(chunk_used))
                dve.wait_ge(*at.done(roped, -1))
                if classes:
                    dve.tensor_tensor(classed(tmp[:, 1, :]), classed(bank[:]), by_class(cosT[:]), ALU.mult)
                else:
                    dve.tensor_tensor(tmp[:, 1, :], bank[:], cosT[:], ALU.mult)
                dve.stream_shuffle(tmp[:, 0, :], bank[:], partner).then_inc(*at.here(acc_free))
                at.passed("rope")

            def turn_over(dst, src, groups):
                dve.wait_ge(*at.done(roped, -1))
                to, from_ = (a[:].rearrange("p (g w) n -> p g w n", g=groups) for a in (dst, src))
                dve.tensor_scalar(to[:, :, 0], from_[:, :, 0], SCORE_SCALE, None, ALU.mult)
                dve.tensor_copy(to[:, :, 1], from_[:, :, 1]).then_inc(*at.here(b_to_a))
                at.passed("turnover")

            def pair_body(attend, proj, pair, mod_col):
                for s in range(10):
                    if proj and s < 9:
                        if s % 3 != 2:
                            rope_read(True)
                        at.passed("chunk")
                        at.passed("bank")
                        if not attend:
                            split_rest()
                    if attend and s < 8:
                        dve.wait_ge(*at.done(s_ready))
                        dve.tensor_reduce(nmax[:, s % 2, 0:1], scores_of(s, proj).rearrange("p b n -> p (b n)")[:, 0:6 * P],
                                          AX.X, ALU.max, negate=True).then_inc(*at.here(maxed))
                        at.passed("unit")
                    if attend and proj and s < 8:
                        split_rest()
                    if attend and 2 <= s <= 9:
                        hh, cls = (s - 2) // 4, (s - 2) % 4
                        unit = -3 if s < 8 else s - 10
                        dve.wait_ge(*at.done(pv_ready, unit))
                        chain(dve.reciprocal(rden[:, 0:1], den[:, cls, 0:1]))
                        dve.tensor_scalar(osb[:, cls, hh * HEAD_DIM:(hh + 1) * HEAD_DIM], pv_acc[:, 0:HEAD_DIM],
                                          rden[:, 0:1], None, ALU.mult).then_inc(*at.here(o_out, unit))
                    if attend and proj and s == 8:
                        split_rest()
                    if attend and 1 <= s <= 8:
                        mod_sum(s - 1)
                if attend:
                    at.passed("tjob", A_TJOBS - 1)
                if proj:
                    turn_over(qkA, qkB, 3)
                if attend:
                    mod_columns(mod_col, 4)
                    mod_columns(mod_col + 4, 4)
                    bank = job_ready()
                    dve.wait_ge(*at.done(s_chain))
                    at.passed("schain")
                    hi, lo = (a[:, bass.ds(pair, 1), :].rearrange("p a (i c) -> p (a c) i", c=CLASSES) for a in (ohi, olo))
                    job_read(dve.tensor_tensor(lo, classed(bank[:]), hi.bitcast(F32), ALU.subtract))

            pair_body(False, True, 0, None)
            with at.loop(PAIRS - 1, chunk=9, bank=9, rope=6, tjob=A_TJOBS + 2, unit=8, turnover=1, mod=DT, schain=1, vchain=8) as turn:
                pair_body(True, True, turn, turn * DT + FFN[0])
            pre_scale(1, FFN[0], PRE_FFN)
            post_gain(1, FFN[0], POST_FFN)
            pair_body(True, False, PAIRS - 1, MIX[0] + 2 * DT)
            def gain_now():
                dve.memset(marks[:, 0:1], 0.0).then_inc(*at.here(gain_ready))
                at.passed("gain")

            def part_of_mean(dt):
                dve.wait_ge(*at.done(s_chain))
                at.passed("schain")
                tile_x, tile_u = (a[:, bass.ds(dt, 1), :].rearrange("p a n -> p (a n)") for a in (xT, yT))
                chain(dve.tensor_tensor(xu_part[:], tile_x, tile_u, ALU.mult))
                dve.tensor_tensor(xu_acc[:], xu_acc[:], xu_part[:], ALU.add).then_inc(*at.here(xu_added))
                at.passed("xu")
                dve.wait_ge(*at.done(xu_added, -1))

            dve.wait_ge(*at.done(t_free, -1))
            post_gain(0, MIX[0], POST_MIX)
            gain_now()
            chain(dve.memset(xu_acc[:], 0.0))

            for q in range(DT // 2):
                part_of_mean(2 * q)
                part_of_mean(2 * q + 1)
                at.passed("chunk")
                split_rest()
                at.passed("bank", 2)
            norms()
            normed(hhi, hlo, 1, FFN[0], update=True)

            def ffn(layer, mods, end):
                def tap(t, ft):
                    return convc[:, bass.ds(ft + (layer * CONV + t * FT), 1)]

                def feature_tile(ft, sums=((), ()), size=1024):
                    bank = acc[at.at("bank", 3)]
                    dve.wait_ge(*at.done(tap_ready))
                    for t, shift in ((1, 1), (0, 2)):
                        conv = tmp[:, 0, shift:T]
                        ins = dve.scalar_tensor_tensor(conv, bank[:, 0:T - shift], tap(t, ft), conv, ALU.mult, ALU.add)
                        if t:
                            chain(ins)
                    ins.then_inc(*at.here(acc_free))
                    at.passed("chunk")
                    at.passed("bank")
                    bank = acc[at.at("bank", 3)]
                    split_rest()
                    for m in sums[0]:
                        mod_sum(m)
                    dve.wait_ge(*at.done(gelu_ready))
                    dve.wait_ge(*at.done(chunk_used))
                    dve.wait_ge(*at.done(g_ready, -1))
                    dve.tensor_tensor(tmp[:, 2, :], bank[:], tmp[:, 1, :], ALU.mult).then_inc(*at.here(acc_free))
                    at.passed("chunk")
                    at.passed("bank")
                    at.passed("ff")
                    split_rest(size=size)
                    for m in sums[1]:
                        mod_sum(m)

                sums = (((), (0,)), ((1,), (2,)), ((3,), ()))
                counts = dict(chunk=6, bank=6, ff=3, vchain=3) | (dict(tjob=2, mod=4) if mods else {})
                with at.loop(MOD_TURNS, **counts) as turn:
                    for j in range(FT_TURN):
                        feature_tile(turn * FT_TURN + j, *([sums[j]] if mods else []))
                    if mods:
                        for q in range(2):
                            mod_columns(turn * 4 + (MIX[1] + 2 * q), 2)
                for j, ft in enumerate(range(MOD_TURNS * FT_TURN, FT)):
                    feature_tile(ft, ((), () if mods else (2 * j, 2 * j + 1)), 1024 if ft < FT - 1 else SHORT)

                def down(dt, sums, last=False):
                    for j in range(3):
                        if j == 2 and not end:
                            part_of_mean(dt)
                        at.passed("chunk")
                        if not (last and end):
                            split_rest(size=SHORT if j == 2 and not last else 1024)
                        if j == 1:
                            for m in sums:
                                mod_sum(m)
                    at.passed("bank")

                if not end:
                    chain(dve.memset(xu_acc[:], 0.0))
                counts = dict(chunk=9, bank=3) | (dict(tjob=2, mod=6) if mods else {}) | ({} if end else dict(schain=3, xu=3, vchain=3))
                with at.loop(DT // 3, **counts) as turn:
                    for j in range(3):
                        down(turn * 3 + j, range(2 * j, 2 * j + 2) if mods else ())
                    if mods:
                        for q in range(2):
                            mod_columns(turn * 6 + (KV + 3 * q), 3)
                if not mods:
                    mod_columns(FFN[1] + 2 * DT, 4)
                    mod_columns(FFN[1] + 2 * DT + 4, 4)
                down(DT - 2, range(2) if mods else ())
                down(DT - 1, range(2, 4) if mods else (), True)
                if mods:
                    for q in range(2):
                        mod_columns(KV + 12 + 2 * q, 2)

            ffn(0, True, False)
            dve.wait_ge(*at.done(t_free, -1))
            pre_scale(2, KV, KVN)
            pre_scale(3, MIX[1], PRE_MIX + DT)
            post_gain(2, MIX[1], POST_MIX + DT)
            norms()
            normed(khi, klo, 2, KV, update=True)
            normed(hhi, hlo, 3, MIX[1])

            def rest_of_o(head):
                bank = job_ready()
                dve.wait_ge(*at.done(s_chain))
                at.passed("schain")
                hi, lo = (a[:, bass.ds(head, 1), :].rearrange("p a n -> p (a n)") for a in (ohi1, olo1))
                job_read(dve.scalar_tensor_tensor(lo, bank[:], small[:, SUBG:SUBG + 1], hi.bitcast(F32), ALU.mult, ALU.subtract))

            def join(n):
                L = (n + 1) * P
                dve.wait_ge(*at.done(exped, -1))
                chain(dve.reciprocal(rden[:], den[:, n, :]))
                chain(dve.tensor_tensor(rden[:, 1:2], rden[:, 1:2], small[:, NEGLAM:NEGLAM + 1], ALU.mult))
                chain(dve.tensor_scalar(prob1[:, 1, 0:L], prob1[:, 1, 0:L], rden[:, 1:2], None, ALU.mult))
                if n >= 2:
                    dve.wait_ge(*at.done(t_ready, -1 if n == 2 else 0))
                dve.scalar_tensor_tensor(aprob[:, n % 2, 0:L], prob1[:, 0, 0:L], rden[:, 0:1], prob1[:, 1, 0:L],
                                         ALU.mult, ALU.add).then_inc(*at.here(joined, -1))

            def head_body(attend, proj, back, head, mod_col=None):
                units = 0
                for s in range(8):
                    if attend and 1 <= s <= 3:
                        join(s - 1)
                    if attend and s < 4:
                        L = (s + 1) * P
                        dve.wait_ge(*at.done(s_ready))
                        dve.tensor_reduce(nmax[:, s % 2, :], scores_of(s, proj)[:, :, 0:L], AX.X, ALU.max, negate=True).then_inc(*at.here(maxed))
                        at.passed("unit")
                        at.passed("unit1")
                        units += 1
                    if proj and s == 5:
                        turn_over(qkA1, qkB1, 1)
                    if proj and s in (1, 3):
                        rope_read(False)
                    if attend and s == 3:
                        join(3)
                    if proj and s in (1, 3, 5):
                        at.passed("chunk")
                        at.passed("bank")
                        split_rest()
                    if attend and s == 0:
                        at.passed("tjob")
                    if back and s == 1:
                        rest_of_o(head)
                    if attend and 2 <= s <= 5:
                        at.passed("tjob")
                    if mod_col is not None and s == 7:
                        mod_columns(mod_col, 1)
                        mod_columns(mod_col + 1, 1)
                    if attend and 4 <= s <= 7:
                        n = s - 4
                        dve.wait_ge(*at.done(o_rms, n - units))
                        dve.tensor_scalar(osb1[:, n, :], oraw[:, n % 2, :], small[:, 28 + n % 2:29 + n % 2], None,
                                          ALU.mult).then_inc(*at.here(o_normed, n - units))
                    if attend and 3 <= s <= 6:
                        n = s - 3
                        dve.wait_ge(*at.done(o_square, n - units))
                        dve.tensor_scalar(small[:, 26 + n % 2:27 + n % 2], small[:, 24 + n % 2:25 + n % 2], 1.0 / P, SUBLN_EPS,
                                          ALU.mult, ALU.add).then_inc(*at.here(o_var, n - units))
                    if mod_col is not None and s == 4:
                        mod_sum(0)
                        mod_sum(1)
            dve.wait_ge(*at.done(h_ready, -1))
            head_body(False, True, False, 0)
            head_body(True, True, False, 0, FFN[1])
            with at.loop(HEADS_B - 2, chunk=3, bank=3, rope=2, tjob=8, unit=4, unit1=4, turnover=1, mod=2, schain=1, vchain=12) as turn:
                head_body(True, True, True, turn, turn * 2 + (FFN[1] + 2))
            head_body(True, False, True, HEADS_B - 2, FFN[1] + 2 * DT - 2)
            rest_of_o(HEADS_B - 1)
            dve.wait_ge(*at.done(t_free, -1))
            pre_scale(4, FFN[1], PRE_FFN + DT)
            gain_now()
            chain(dve.memset(xu_acc[:], 0.0))
            for dt in range(DT):
                part_of_mean(dt)
                at.passed("chunk")
                split_rest()
                at.passed("bank")
            norms()
            normed(hhi, hlo, 4, FFN[1], update=True)
            ffn(1, False, True)
            factors()
            post_gain(3, FFN[1], POST_FFN + DT)
            update_x(3)
            for j in range(8):
                half, t = j // 4, j % 4
                if j % 2 == 0:
                    bank = job_ready()
                    dve.tensor_copy(otok[:, t, half * 512:half * 512 + 512], bank[:]).then_inc(*at.here(out_ready))
                at.passed("otile")
                at.passed("tjob")

        @block.gpsimd
        def _(pool):
            at = Count(pool)

            def chain(ins):
                ins.then_inc(*at.here(g_chain))
                pool.wait_ge(*at.done(g_chain))
                at.passed("gchain")

            def select(ap, pattern, base, per_partition, fill, compare=ALU.is_ge):
                return pool.affine_select(out=ap, in_=ap, compare_op=compare, fill=fill, base=base,
                                          pattern=pattern, channel_multiplier=per_partition)

            chain(pool.memset(onesf[:], 1.0))
            chain(pool.memset(neghalf[:], -0.5))
            chain(pool.memset(identf[:], 0.0))
            select(identf[:], [[-1, P]], 0, 1, 1.0, ALU.not_equal).then_inc(*at.here(consts_ready))
            chain(pool.memset(sqacc[:], 0.0))
            pool.iota(tmp[:, 3, 0:P].bitcast(I32), pattern=[[-1, P]], base=P, channel_multiplier=1).then_inc(*at.here(diffs_ready))
            reach = WINDOW // CLASSES
            chain(pool.memset(band[:], 0.0))
            chain(pool.memset(causal[:], 0.0))
            chain(pool.memset(near[:, 0:P], 0.0))
            for b0, n, low, high in ((0, 3, 0, reach - 1), (3, 1, 0, reach), (4, 3, 1, reach)):
                part = band[:, b0 * P:(b0 + n) * P].rearrange("p (b k) -> p b k", k=P)
                chain(select(part, [[0, n], [-1, P]], -low, 1, MASKED))
                chain(select(part, [[0, n], [1, P]], high, -1, MASKED))
            chain(select(causal[:, 3 * P:4 * P], [[-1, P]], 0, 1, MASKED))
            pool.wait_ge(*at.done(near_ready))
            select(near[:].rearrange("p (b k) -> p b k", k=P), [[0, 2], [-1, P]], 0, 1, MASKED).then_inc(*at.here(masks_ready))

            def power(dst):
                pool.tensor_tensor(dst, STAT_V, neghalf[:], ALU.pow).then_inc(*at.here(stat_r))
                at.passed("stat")

            def factors():
                pool.wait_ge(*at.done(t_free))
                at.passed("tjob", 2)
                power(STAT_R)

            def norms():
                pool.wait_ge(*at.done(t_free))
                power(STAT_R)
                pool.wait_ge(*at.done(mean_ready))
                at.passed("mean")
                power(STAT_Q)
                pool.wait_ge(*at.done(t_free, 2))
                at.passed("tjob", 4)
                for k in range(1, DT, 2):
                    chain(pool.tensor_tensor(yT[:, k, :], yT[:, k, :], fb[:], ALU.mult))
                    pool.tensor_tensor(xT[:, k, :], xT[:, k, :], yT[:, k, :], ALU.add).then_inc(*at.here(x_odd))
                    at.passed("xo")
                chain(pool.memset(sqacc[:], 0.0))

            def scale_mod(ap):
                return pool.tensor_tensor(ap, ap, csil[:].rearrange("p (k a) -> p k a", a=1).to_broadcast([P, DT, P]), ALU.mult)

            pool.wait_ge(*at.done(c_ready))
            for n, j in enumerate(DVE_MODS):
                pool.wait_ge(*at.done(mods_landed[j]))
                scale_mod(mstart[:, j, :, 0:P]).then_inc(*at.here(m0_scaled))
                at.passed("m0_scaled")
                if n == 1:
                    pool.wait_ge(*at.done(mean_ready))
                    at.passed("mean")
                    power(STAT_R)
            at.passed("tjob", 2 + DT + 3 + len(PE_MODS) + 4)

            fetched = [0]

            def fetch_mod(w, col):
                event = fetched[0]
                pool.wait_ge(*at.done(m_summed, event - 2))
                slot = (at.at("mod", 2) + event) % 2
                pool.dma_start(mraw[:, slot], w[:, bass.ds(col, P)].rearrange("(k p) n -> p k n", p=P)).then_inc(*at.here(m_landed, event))
                fetched[0] += 1

            def mod_step():
                pool.wait_ge(*at.done(m_landed))
                scale_mod(mraw[:, at.at("mod", 2)]).then_inc(*at.here(m_scaled))
                at.passed("mod")
                fetched[0] -= 1

            def rope_write(dst, classes):
                pool.wait_ge(*at.done(acc_free))
                part = tmp[:, 0, :]
                if classes:
                    chain(pool.tensor_tensor(classed(part), classed(part), by_class(sinT[:]), ALU.mult))
                else:
                    chain(pool.tensor_tensor(part, part, sinT[:], ALU.mult))
                pool.tensor_tensor(dst, part, tmp[:, 1, :], ALU.add).then_inc(*at.here(roped))
                at.passed("rope")

            def pair_body(proj, w=None, col=None):
                if proj:
                    pool.wait_ge(*at.done(b_to_a, -1))
                for s in range(9):
                    if w is not None and s < DT:
                        fetch_mod(w, col + s * P)
                    if w is not None and s > 0:
                        mod_step()
                    g, kind = KINDS[s]
                    if proj and kind != 2:
                        rope_write(qkB[:, 2 * g + kind, :], True)
                    if proj:
                        at.passed("bank")
                if proj:
                    at.passed("turnover")

            pool.wait_ge(*at.done(tables_ready))
            pair_body(True)
            with at.loop(PAIRS - 1, bank=9, rope=6, turnover=1, mod=DT, gchain=6) as turn:
                pair_body(True, mod_ffn_w[0], turn * D)
            pair_body(False, mod_mix_w[0], 2 * D)
            at.passed("tjob", PAIRS * (A_TJOBS + 2))

            def add_square(slot, last=False):
                pool.wait_ge(*at.done(y_squared))
                pool.wait_ge(*at.done(sq_added, -1))
                pool.tensor_tensor(sqacc[:], sqacc[:], tmp[:, slot, :], ALU.add).then_inc(*at.here(sq_added))
                if not last:
                    pool.wait_ge(*at.done(acc_free))
                    pool.wait_ge(*at.done(uu_added, -1))
                    pool.tensor_tensor(uu_acc[:], uu_acc[:], uu_part[:, slot, :], ALU.add).then_inc(*at.here(uu_added))
                    at.passed("uu")
                at.passed("bank")
                at.passed("ysq")

            def update_x():
                for k in range(DT):
                    if k % 2:
                        pool.wait_ge(*at.done(y_scaled))
                        pool.tensor_tensor(xT[:, k, :], xT[:, k, :], yT[:, k, :], ALU.add).then_inc(*at.here(x_odd))
                        at.passed("xo")
                    at.passed("yx")

            chain(pool.memset(uu_acc[:], 0.0))
            for dt in range(DT):
                add_square(dt % 3)
            norms()

            def ffn(mods):
                def feature_tile(ft, j=None, col=None):
                    if j is not None:
                        mods_of_half(2 * j, col)
                    pool.wait_ge(*at.done(g_hi))
                    pool.tensor_tensor(glo[:, bass.ds(ft, 1), :].rearrange("p a n -> p (a n)"), tmp[:, 2, :],
                                       ghi[:, bass.ds(ft, 1), :].rearrange("p a n -> p (a n)").bitcast(F32),
                                       ALU.subtract).then_inc(*at.here(g_ready))
                    at.passed("ff")
                    at.passed("bank", 2)
                    if j is not None:
                        mods_of_half(2 * j + 1, col)

                def mods_of_half(half, col):
                    if 1 <= half <= 4:
                        mod_step()
                    for m in ((0, 1), (), (2, 3), (), (), ())[half]:
                        fetch_mod(mod_mix_w[1], col + m * P)

                def two_mods(col):
                    if mods:
                        fetch_mod(kv_mod_w, col)
                        fetch_mod(kv_mod_w, col + P)
                        mod_step()
                        mod_step()

                with at.loop(MOD_TURNS, bank=6, ff=3, **(dict(mod=4) if mods else {})) as turn:
                    for j in range(FT_TURN):
                        feature_tile(turn * FT_TURN + j, *((j, turn * (4 * P)) if mods else ()))
                if mods:
                    at.passed("tjob", 2 * MOD_TURNS)
                for ft in range(MOD_TURNS * FT_TURN, FT):
                    if not mods:
                        col = 2 * D + 2 * (ft - MOD_TURNS * FT_TURN) * P
                        fetch_mod(mod_ffn_w[1], col)
                        fetch_mod(mod_ffn_w[1], col + P)
                    feature_tile(ft)
                    if not mods:
                        mod_step()
                        mod_step()
                if mods:
                    chain(pool.memset(uu_acc[:], 0.0))
                with at.loop(DT // 3, bank=3, ysq=3, **(dict(mod=6, uu=3) if mods else {})) as turn:
                    for j in range(3):
                        two_mods(turn * (6 * P) + 2 * j * P)
                        add_square(j, not mods)
                for dt in range(DT // 3 * 3, DT):
                    two_mods(2 * dt * P)
                    add_square(dt % 3, not mods)
                at.passed("tjob", 6 if mods else 2)

            ffn(True)
            norms()

            def head_body(attend, proj, col):
                if proj:
                    pool.wait_ge(*at.done(b_to_a, -1))
                units = 0
                for s in range(7):
                    if attend and s == 0:
                        fetch_mod(mod_ffn_w[1], col)
                        fetch_mod(mod_ffn_w[1], col + P)
                    if proj and s in (1, 3):
                        rope_write(qkB1[:, 1 if s == 1 else 0, :], False)
                    if attend and s == 2:
                        mod_step()
                        mod_step()
                    if proj and s in (1, 3, 5):
                        at.passed("bank")
                    if attend and s < 4:
                        at.passed("unit1")
                        units += 1
                    if attend and 3 <= s <= 6:
                        n = s - 3
                        pool.wait_ge(*at.done(o_var, n - units))
                        pool.tensor_tensor(small[:, 28 + n % 2:29 + n % 2], small[:, 26 + n % 2:27 + n % 2], neghalf[:, 0:1],
                                           ALU.pow).then_inc(*at.here(o_rms, n - units))
                if proj:
                    at.passed("turnover")

            head_body(False, True, None)
            head_body(True, True, 0)
            with at.loop(HEADS_B - 2, bank=3, rope=2, unit1=4, turnover=1, mod=2, gchain=2) as turn:
                head_body(True, True, turn * (2 * P) + 2 * P)
            head_body(True, False, (2 * DT - 2) * P)
            at.passed("tjob", 7 + 8 * (HEADS_B - 2) + 8 + 1)
            chain(pool.memset(uu_acc[:], 0.0))
            for dt in range(DT):
                add_square(dt % 3)
            norms()
            ffn(False)
            factors()
            update_x()


_INS = ['x', 'c', 'positions', 'mod_mix_w', 'mod_mix_b', 'mod_ffn_w', 'mod_ffn_b',
        'norm_pre_mix', 'norm_post_mix', 'norm_pre_ffn', 'norm_post_ffn',
        'ffn_w_gate', 'ffn_w_up', 'ffn_conv_w', 'ffn_conv_b', 'ffn_w_down',
        'a_w_qkv', 'a_w_o', 'kv_norm', 'kv_mod_w', 'kv_mod_b', 'b_w_k', 'b_w_v',
        'b_w_q', 'b_lambda_q1', 'b_lambda_k1', 'b_lambda_q2', 'b_lambda_k2', 'b_subln', 'b_w_o']
_OUT = ((1, 512, 1024), 'float32')


def kernel(**inputs):
    import numpy as _np
    import concourse.bacc as _bacc
    from concourse import mybir as _mybir
    from concourse.bass_utils import run_bass_kernel_spmd as _run

    nc = _bacc.Bacc("TRN2", target_bir_lowering=False, num_devices=1)
    arrays, args = {}, []
    for name in _INS:
        a = _np.ascontiguousarray(inputs[name])
        arrays[f"in_{name}_dram"] = a
        args.append(nc.dram_tensor(f"in_{name}_dram", a.shape, _mybir.dt.from_np(a.dtype), kind="ExternalInput").ap())
    args.append(nc.dram_tensor("out_0_dram", _OUT[0], _mybir.dt.from_np(_np.dtype(_OUT[1])), kind="ExternalOutput").ap())
    yoco_trunk(nc, *args)
    r = _run(nc, [arrays], core_ids=[0])
    return r.results[0]["out_0_dram"]
```
